# Optimizing a Trainium2 kernel written in Bass

```python
import jax, jax.numpy as jnp
from jax import lax
import numpy as np

D_MODEL = 1024
BATCH = 1
SEQ = 2048
DEPTH = 1
DEC_BATCH = 8
DEC_SEQ = 8
PAST_LEN = 8192
PAGE_SIZE = 128

PLE_DIM = 256
NORM_EPS = 1e-6
GLA_HEADS = 4
GLA_DK = D_MODEL // 2 // GLA_HEADS
GLA_DV = D_MODEL // GLA_HEADS
GLA_KEY = GLA_HEADS * GLA_DK
GLA_VAL = GLA_HEADS * GLA_DV
GLA_LOWRANK = 16
GLA_TAU = 16.0
GLA_CHUNK = 64
DIL_GROUPS = ((128, 1), (512, 4), (2048, 16))
DIL_HEADS = 4
DIL_HD = 128
DIL_WIDTH = DIL_HEADS * DIL_HD
DIL_QKV = len(DIL_GROUPS) * DIL_WIDTH
IN_SPLITS = (GLA_KEY, GLA_KEY, GLA_VAL, GLA_VAL, GLA_LOWRANK,
             DIL_QKV, DIL_QKV, DIL_QKV, DIL_WIDTH, D_MODEL, D_MODEL)
IN_WIDTH = sum(IN_SPLITS)

kernel_name = "gla_dilated_window_gated_hybrid_step"

def _rmsnorm(x, g):
    xf = x.astype(jnp.float32)
    y = xf * lax.rsqrt(jnp.mean(xf * xf, axis=-1, keepdims=True) + NORM_EPS)
    return (y * g.astype(jnp.float32)).astype(x.dtype)

def _gla(q, k, v, log_a, s0):
    f32 = jnp.float32
    B, L, H, DK = q.shape
    DV = v.shape[-1]
    C = min(GLA_CHUNK, L)
    n = -(-L // C)
    pad = n * C - L

    def chunks(t):
        t = jnp.pad(t.astype(f32), ((0, 0), (0, pad), (0, 0), (0, 0)))
        return jnp.moveaxis(t.reshape(B, n, C, H, t.shape[-1]), 1, 0)

    qc, kc, vc, ac = chunks(q), chunks(k), chunks(v), chunks(log_a)
    causal = jnp.tril(jnp.ones((C, C), dtype=bool))

    def step(s, inp):
        q_, k_, v_, a_ = inp
        b = jnp.cumsum(a_, axis=1)
        b_end = b[:, -1]
        q_in = q_ * jnp.exp(b)
        att = jnp.einsum('bihd,bjhd->bhij', q_in, k_ * jnp.exp(-b))
        att = jnp.where(causal, att, 0.0)
        o = (jnp.einsum('bhij,bjhe->bihe', att, v_)
             + jnp.einsum('bihd,bhde->bihe', q_in, s))
        k_end = k_ * jnp.exp(b_end[:, None] - b)
        s = jnp.exp(b_end)[..., None] * s + jnp.einsum('bjhd,bjhe->bhde', k_end, v_)
        return s, o

    s_fin, o = lax.scan(step, s0.astype(f32), (qc, kc, vc, ac))
    o = jnp.moveaxis(o, 0, 1).reshape(B, n * C, H, DV)[:, :L]
    return o, s_fin

def _dilated_prompt(q, k, v, dil, span):
    f32 = jnp.float32
    B, S, H, D = q.shape
    L = S // dil
    nb = -(-L // span)

    def split(t):
        t = t.astype(f32).reshape(B, L, dil, H, D)
        t = jnp.pad(t, ((0, 0), (0, nb * span - L), (0, 0), (0, 0), (0, 0)))
        return t.reshape(B, nb, span, dil, H, D)

    qs, ks, vs = split(q), split(k), split(v)

    def with_prev(t):
        prev = jnp.pad(t, ((0, 0), (1, 0), (0, 0), (0, 0), (0, 0), (0, 0)))[:, :-1]
        return jnp.concatenate([prev, t], axis=2)

    kk, vv = with_prev(ks), with_prev(vs)
    i = span + jnp.arange(span)[:, None]
    j = jnp.arange(2 * span)[None, :]
    band = (i - j >= 0) & (i - j <= span)
    first = (jnp.arange(nb)[:, None, None] == 0) & (j < span)[None]
    valid = (band[None] & ~first)[None, :, None, None]
    s = jnp.einsum('bnirhd,bnjrhd->bnrhij', qs, kk) * (D ** -0.5)
    s = jnp.where(valid, s, -jnp.inf)
    m = jnp.max(s, axis=-1, keepdims=True)
    p = jnp.exp(s - m)
    l = jnp.sum(p, axis=-1, keepdims=True)
    o = jnp.einsum('bnrhij,bnjrhd->bnirhd', p / l, vv)
    lse = jnp.moveaxis((m + jnp.log(l))[..., 0], -1, 2)
    o = o.reshape(B, nb * span, dil, H, D)[:, :L].reshape(B, S, H, D)
    lse = lse.reshape(B, nb * span, dil, H)[:, :L].reshape(B, S, H)
    return o, lse

def _dilated_sample(q, k, v, buf, dil, span):
    f32 = jnp.float32
    B, T, H, D = q.shape
    Lb = buf.shape[1]
    kk = jnp.concatenate([buf[:, :, 0].astype(f32), k.astype(f32)], axis=1)
    vv = jnp.concatenate([buf[:, :, 1].astype(f32), v.astype(f32)], axis=1)
    idx = Lb + jnp.arange(T)[:, None] - dil * jnp.arange(span + 1)[None, :]
    valid = (idx >= 0)[None, :, None, :]
    idx = jnp.maximum(idx, 0)
    kg = jnp.take(kk, idx, axis=1)
    vg = jnp.take(vv, idx, axis=1)
    s = jnp.einsum('bthd,btkhd->bthk', q.astype(f32), kg) * (D ** -0.5)
    s = jnp.where(valid, s, -jnp.inf)
    m = jnp.max(s, axis=-1, keepdims=True)
    p = jnp.exp(s - m)
    l = jnp.sum(p, axis=-1, keepdims=True)
    o = jnp.einsum('bthk,btkhd->bthd', p / l, vg)
    lse = (m + jnp.log(l))[..., 0]
    keep = min(dil * span, Lb + T)
    new_buf = jnp.stack([kk, vv], axis=2)[:, Lb + T - keep:].astype(buf.dtype)
    return o, lse, new_buf

def _layer(x, pe, gla_s0, bufs, g_pre, g_post, w_in, w_gla_lr, b_gla_lr, g_gla_norm,
           w_gla_branch, w_dil_branch, w_out, w_ple_proj, w_ple_gate):
    B, L, _ = x.shape
    xn = _rmsnorm(x, g_pre)
    u = xn @ w_in
    cuts = np.cumsum(IN_SPLITS)[:-1].tolist()
    gq, gk, gv, gg, glr, dq, dk, dv, dg, ga, gb = jnp.split(u, cuts, axis=-1)

    q = gq.reshape(B, L, GLA_HEADS, GLA_DK) * (GLA_DK ** -0.5)
    k = gk.reshape(B, L, GLA_HEADS, GLA_DK)
    v = gv.reshape(B, L, GLA_HEADS, GLA_DV)
    z = (glr @ w_gla_lr + b_gla_lr).astype(jnp.float32)
    log_a = (jax.nn.log_sigmoid(z) / GLA_TAU).reshape(B, L, GLA_HEADS, GLA_DK)
    o_a, s_new = _gla(q, k, v, log_a, gla_s0)
    o_a = _rmsnorm(o_a.astype(x.dtype), g_gla_norm.reshape(GLA_HEADS, GLA_DV)).reshape(B, L, GLA_VAL)
    y_a = (o_a * jax.nn.silu(gg)) @ w_gla_branch

    ng = len(DIL_GROUPS)
    dq = dq.reshape(B, L, ng, DIL_HEADS, DIL_HD)
    dk = dk.reshape(B, L, ng, DIL_HEADS, DIL_HD)
    dv = dv.reshape(B, L, ng, DIL_HEADS, DIL_HD)
    outs, lses, new_bufs = [], [], []
    for g, (win, dil) in enumerate(DIL_GROUPS):
        span = win // dil
        qg, kg, vg = dq[:, :, g], dk[:, :, g], dv[:, :, g]
        if bufs is None:
            o_g, lse_g = _dilated_prompt(qg, kg, vg, dil, span)
            keep = min(win, L)
            nbuf = jnp.stack([kg, vg], axis=2)[:, L - keep:]
        else:
            o_g, lse_g, nbuf = _dilated_sample(qg, kg, vg, bufs[g], dil, span)
        outs.append(o_g)
        lses.append(lse_g)
        new_bufs.append(nbuf)
    wts = jax.nn.softmax(jnp.stack(lses), axis=0)
    o_b = jnp.einsum('gblh,gblhd->blhd', wts, jnp.stack(outs)).reshape(B, L, DIL_WIDTH)
    y_b = (o_b.astype(x.dtype) * jax.nn.silu(dg)) @ w_dil_branch

    merged = jax.nn.sigmoid(ga) * y_a + jax.nn.sigmoid(gb) * y_b
    h = x + _rmsnorm(merged @ w_out, g_post)
    h = h + (pe @ w_ple_proj) * jax.nn.sigmoid(h @ w_ple_gate)
    return h, s_new.astype(x.dtype), new_bufs

def setup_inputs(seed: int = 0) -> dict:
    key = jax.random.key(seed)
    ks = jax.random.split(key, 24)
    f32 = jnp.float32
    nrm = lambda k, shape, sc: jax.random.normal(k, shape, f32) * sc
    buf_len = [min(w, PAST_LEN) for (w, _) in DIL_GROUPS]
    return {
        "x_prompt": nrm(ks[0], (BATCH, SEQ, D_MODEL), 1.0),
        "x_sample": nrm(ks[1], (DEC_BATCH, DEC_SEQ, D_MODEL), 1.0),
        "state_gla": nrm(ks[2], (DEPTH, DEC_BATCH, GLA_HEADS, GLA_DK, GLA_DV), 1.0),
        "cache_kv_w128": nrm(ks[3], (DEPTH, DEC_BATCH, buf_len[0], 2, DIL_HEADS, DIL_HD), 1.0),
        "cache_kv_w512": nrm(ks[4], (DEPTH, DEC_BATCH, buf_len[1], 2, DIL_HEADS, DIL_HD), 1.0),
        "cache_kv_w2048": nrm(ks[5], (DEPTH, DEC_BATCH, buf_len[2], 2, DIL_HEADS, DIL_HD), 1.0),
        "p_prompt": nrm(ks[6], (DEPTH, BATCH, SEQ, PLE_DIM), 1.0),
        "p_sample": nrm(ks[7], (DEPTH, DEC_BATCH, DEC_SEQ, PLE_DIM), 1.0),
        "g_pre": 1.0 + nrm(ks[8], (DEPTH, D_MODEL), 0.02),
        "g_post": 1.0 + nrm(ks[9], (DEPTH, D_MODEL), 0.02),
        "w_in": nrm(ks[10], (DEPTH, D_MODEL, IN_WIDTH), D_MODEL ** -0.5),
        "w_gla_lr": nrm(ks[11], (DEPTH, GLA_LOWRANK, GLA_KEY), GLA_LOWRANK ** -0.5),
        "b_gla_lr": nrm(ks[12], (DEPTH, GLA_KEY), 0.02),
        "g_gla_norm": 1.0 + nrm(ks[13], (DEPTH, GLA_VAL), 0.02),
        "w_gla_branch": nrm(ks[14], (DEPTH, GLA_VAL, D_MODEL), GLA_VAL ** -0.5),
        "w_dil_branch": nrm(ks[15], (DEPTH, DIL_WIDTH, D_MODEL), DIL_WIDTH ** -0.5),
        "w_out": nrm(ks[16], (DEPTH, D_MODEL, D_MODEL), D_MODEL ** -0.5),
        "w_ple_proj": nrm(ks[17], (DEPTH, PLE_DIM, D_MODEL), PLE_DIM ** -0.5),
        "w_ple_gate": nrm(ks[18], (DEPTH, D_MODEL, D_MODEL), D_MODEL ** -0.5),
    }

def reference(x_prompt, x_sample, state_gla, cache_kv_w128, cache_kv_w512, cache_kv_w2048,
              p_prompt, p_sample, g_pre, g_post, w_in, w_gla_lr, b_gla_lr, g_gla_norm,
              w_gla_branch, w_dil_branch, w_out, w_ple_proj, w_ple_gate):
    hp, hs = x_prompt, x_sample
    gla_p, gla_s = [], []
    kvp = [[], [], []]
    kvs = [[], [], []]
    for i in range(DEPTH):
        lw = (g_pre[i], g_post[i], w_in[i], w_gla_lr[i], b_gla_lr[i], g_gla_norm[i],
              w_gla_branch[i], w_dil_branch[i], w_out[i], w_ple_proj[i], w_ple_gate[i])
        s0 = jnp.zeros((x_prompt.shape[0], GLA_HEADS, GLA_DK, GLA_DV), x_prompt.dtype)
        hp, sp_new, bp_new = _layer(hp, p_prompt[i], s0, None, *lw)
        hs, ss_new, bs_new = _layer(hs, p_sample[i], state_gla[i],
                                    (cache_kv_w128[i], cache_kv_w512[i], cache_kv_w2048[i]), *lw)
        gla_p.append(sp_new)
        gla_s.append(ss_new)
        for g in range(len(DIL_GROUPS)):
            kvp[g].append(bp_new[g])
            kvs[g].append(bs_new[g])
    state_gla_prompt = jnp.stack(gla_p)
    state_gla_sample = jnp.stack(gla_s)
    kv_w128_prompt, kv_w512_prompt, kv_w2048_prompt = (jnp.stack(kvp[0]), jnp.stack(kvp[1]), jnp.stack(kvp[2]))
    kv_w128_sample, kv_w512_sample, kv_w2048_sample = (jnp.stack(kvs[0]), jnp.stack(kvs[1]), jnp.stack(kvs[2]))
    return (hp, hs, state_gla_prompt, state_gla_sample,
            kv_w128_prompt, kv_w512_prompt, kv_w2048_prompt,
            kv_w128_sample, kv_w512_sample, kv_w2048_sample)


_drawn_inputs = setup_inputs


def setup_inputs(seed=0):
    import zlib

    import numpy as np

    out = dict(_drawn_inputs(seed))
    spreads = {}
    factors = {'g_post': 4.255, 'b_gla_lr': 6.569, 'g_gla_norm': 4.157}
    for name, (base, spread) in spreads.items():
        noise = np.random.default_rng([zlib.crc32(name.encode()), seed]).standard_normal(out[name].shape)
        drawn = base * np.exp(spread * noise) if base else spread * noise
        out[name] = __import__('jax').numpy.asarray(drawn.astype(out[name].dtype))
    for name, factor in factors.items():
        out[name] = (out[name] * factor).astype(out[name].dtype)
    return out
```

```python
from contextlib import ExitStack

import numpy as np

import concourse.bass as bass
from concourse import mybir

F32 = mybir.dt.float32
F16 = mybir.dt.float16
ALU = mybir.AluOpType
ACT = mybir.ActivationFunctionType
AX_X = mybir.AxisListType.X

P = 128
BANK = 512
D_MODEL = 1024
SEQ = 2048
DEC_BATCH = 8
DEC_SEQ = 8
SAMPLES = DEC_BATCH * DEC_SEQ
TOKENS = SEQ + SAMPLES
TOKEN_TILES = -(-TOKENS // P)
K_TILES = D_MODEL // P
NORM_EPS = 1e-6

HEADS = 4
GLA_DK = 128
GLA_DV = 256
GLA_KEY = HEADS * GLA_DK
GLA_VAL = HEADS * GLA_DV
LOWRANK = 16
GLA_TAU = 16.0
GLA_CHUNK = 64

HD = 128
WIDTH = HEADS * HD
WINDOWS = ((128, 1), (512, 4), (2048, 16))
GROUPS = len(WINDOWS)
SPAN = 128
BLOCKS = SEQ // SPAN
SCALE = float(HD) ** -0.5
MASKED = -1e30

PLE = 256

W_LOWRANK = 2 * GLA_KEY + 2 * GLA_VAL
U_GQ = 0
U_GK = GLA_KEY
U_GV = 2 * GLA_KEY
U_GG = U_GV + GLA_VAL
U_DQ = U_GG + GLA_VAL
U_DK = U_DQ + GROUPS * WIDTH
U_DV = U_DK + GROUPS * WIDTH
U_DG = U_DV + GROUPS * WIDTH
U_GA = U_DG + WIDTH
U_GB = U_GA + D_MODEL
U_WIDTH = U_GB + D_MODEL
COLUMN_TILES = U_WIDTH // BANK
TILES_BEFORE_LOWRANK = W_LOWRANK // BANK

W_SCALE = 64.0

START = 1


def apart(eng):
    eng.nop(nofuse=True)


class Core:

    def __init__(self, nc):
        self.nc = nc

    def clear(self, sems):
        if sems:
            self.nc.clear_and_free_semaphores(sems)
            self.nc.all_engine_barrier()

    def bind(self, ctx, prefix=""):
        nc = self.nc
        sems = []
        ctx.callback(self.clear, sems)

        def sb(name, shape, dt=F32):
            return ctx.enter_context(nc.sbuf_tensor(prefix + name, shape, dt))

        def sem(name, start=START):
            sems.append(nc.alloc_semaphore(name=prefix + name))
            if start:
                nc.gpsimd.sem_inc(sems[-1], start)
            return sems[-1]

        def banks(name):
            return [ctx.enter_context(nc.psum_tensor(f"{prefix}{name}{b}", [P, BANK], F32)) for b in range(8)]

        return sb, sem, banks


def normalize_inputs(core, x_prompt, x_sample, g_pre, w_view, raw, raw_loaded, identity, xn_hi, xn_lo):
    nc = core.nc
    with ExitStack() as ctx:
        sb, sem, banks = core.bind(ctx)
        TILES = BANK // P
        x = [sb(f"x{s}", [P, TILES, D_MODEL]) for s in range(2)]
        squares = [sb(f"squares{s}", [P, D_MODEL]) for s in range(2)]
        g = sb("g", [P, K_TILES])
        mean = [sb(f"mean{s}", [P, TILES]) for s in range(2)]
        power = sb("power", [P, TILES])
        guarded = [sb(f"guarded{s}", [P, TILES]) for s in range(2)]
        rstd = [sb(f"rstd{s}", [P, TILES]) for s in range(2)]
        turned = banks("turned")
        g_loaded = sem("g_loaded")
        x_loaded = [[sem(f"x_loaded{s}{t}") for t in range(TILES)] for s in range(2)]
        squared = sem("squared")
        power_ready = sem("power_ready")
        guarded_ready = sem("guarded_ready")
        rstd_ready = sem("rstd_ready")
        scaled = sem("scaled")
        turned_ready = sem("turned_ready")
        hi_ready = sem("hi_ready")
        lo_ready = sem("lo_ready")
        ident_zero = sem("ident_zero")
        ident_ready = sem("ident_ready")
        GROUPS_X = [(TILES, P)] * (SEQ // BANK) + [(1, SAMPLES)]
        nc.all_engine_barrier()
        block = ctx.enter_context(nc.Block())

        def wait(eng, sem, n):
            if n > 0:
                eng.wait_ge(sem, START + n)

        @block.sync
        def _(sp):
            for i, (tiles, rows) in enumerate(GROUPS_X):
                wait(sp, turned_ready, (i - 1) * K_TILES)
                for t in range(tiles):
                    src = x_sample.rearrange("b t d -> (b t) d") if rows < P else x_prompt[0, i * BANK + t * P:i * BANK + (t + 1) * P, :]
                    sp.dma_start(x[i % 2][:rows, t, :], src).then_inc(x_loaded[i % 2][t], 16)
                if i == 0:
                    with nc.allow_non_contiguous_dma(reason="gains, once"):
                        sp.dma_start(g[:, :], g_pre[0].rearrange("(k p) -> p k", p=P)).then_inc(g_loaded, 16)
            for s in range(2):
                sp.dma_start(raw[s][:, :, :], w_view[:, :, s * BANK:(s + 1) * BANK]).then_inc(raw_loaded[s], 16)

        @block.gpsimd
        def _(pool):
            pool.memset(identity[:, :], 0.0).then_inc(ident_zero, 1)
            pool.wait_ge(ident_zero, START + 1)
            pool.affine_select(out=identity[:, :], in_=identity[:, :], compare_op=ALU.not_equal, fill=1.0,
                               base=0, pattern=[[-1, P]], channel_multiplier=1).then_inc(ident_ready, 1)
            pool.memset(power[:, :], -0.5).then_inc(power_ready, 1)
            pool.wait_ge(power_ready, START + 1)
            for i, (tiles, rows) in enumerate(GROUPS_X):
                s = i % 2
                pool.wait_ge(squared, START + i * TILES + tiles)
                pool.tensor_scalar(guarded[s][:rows, :tiles], mean[s][:rows, :tiles], NORM_EPS, None,
                                   ALU.add).then_inc(guarded_ready, 1)
                pool.wait_ge(guarded_ready, START + i + 1)
                wait(pool, scaled, (i - 1) * TILES)
                pool.tensor_tensor(rstd[s][:rows, :tiles], guarded[s][:rows, :tiles], power[:rows, :tiles],
                                   ALU.pow).then_inc(rstd_ready, 1)

        @block.scalar
        def _(act):
            def square(i):
                tiles, rows = GROUPS_X[i]
                wait(act, guarded_ready, i - 1)
                for t in range(tiles):
                    act.wait_ge(x_loaded[i % 2][t], START + (i // 2 + 1) * 16)
                    wait(act, squared, i * TILES + t - 1)
                    act.activation(squares[t % 2][:rows, :], x[i % 2][:rows, t, :], ACT.Square, scale=D_MODEL ** -0.5,
                                   accum_out=mean[i % 2][:rows, t:t + 1]).then_inc(squared, 1)

            square(0)
            act.wait_ge(g_loaded, START + 16)
            for i, (tiles, rows) in enumerate(GROUPS_X):
                if i + 1 < len(GROUPS_X):
                    square(i + 1)
                n = (tiles - 1) * P + rows
                for k in range(K_TILES):
                    act.wait_ge(turned_ready, START + i * K_TILES + k + 1)
                    act.activation(xn_hi[:, k, i * BANK:i * BANK + n], turned[k][:, :n], ACT.Copy,
                                   scale=g[:, k:k + 1]).then_inc(hi_ready, 1)

        @block.vector
        def _(dve):
            def scale(i):
                tiles, rows = GROUPS_X[i]
                dve.wait_ge(rstd_ready, START + i + 1)
                for t in range(tiles):
                    dve.tensor_scalar(x[i % 2][:rows, t, :], x[i % 2][:rows, t, :], rstd[i % 2][:rows, t:t + 1], None,
                                      ALU.mult).then_inc(scaled, 1)

            scale(0)
            dve.wait_ge(g_loaded, START + 16)
            for i, (tiles, rows) in enumerate(GROUPS_X):
                if i + 1 < len(GROUPS_X):
                    scale(i + 1)
                n = (tiles - 1) * P + rows
                for k in range(K_TILES):
                    dve.wait_ge(hi_ready, START + i * K_TILES + k + 1)
                    dve.scalar_tensor_tensor(out=xn_lo[:, k, i * BANK:i * BANK + n], in0=turned[k][:, :n],
                                             scalar=g[:, k:k + 1], in1=xn_hi[:, k, i * BANK:i * BANK + n],
                                             op0=ALU.mult, op1=ALU.subtract).then_inc(lo_ready, 1)

        @block.tensor
        def _(pe):
            pe.wait_ge(ident_ready, START + 1)
            for i, (tiles, rows) in enumerate(GROUPS_X):
                pe.wait_ge(scaled, START + i * TILES + tiles)
                for k in range(K_TILES):
                    wait(pe, lo_ready, (i - 1) * K_TILES + k + 1)
                    for t in range(tiles):
                        last = pe.transpose(turned[k][:, t * P:t * P + rows], x[i % 2][:rows, t, k * P:(k + 1) * P],
                                            identity[:rows, :rows])
                    last.then_inc(turned_ready, 1)


def project_inputs(core, w_view, w_lr, b_lr, raw, raw_loaded, xn_hi, xn_lo, U, lowrank, decay_w, shift_cache):
    nc = core.nc
    with ExitStack() as ctx:
        sb, sem, banks = core.bind(ctx)
        w_hi = [sb(f"w_hi{s}", [P, K_TILES, BANK], F16) for s in range(2)]
        w_lo = [sb(f"w_lo{s}", [P, K_TILES, BANK], F16) for s in range(2)]
        glr = sb("glr", [P, K_TILES, LOWRANK])
        glr_hi = sb("glr_hi", [P, K_TILES, LOWRANK], F16)
        glr_lo = sb("glr_lo", [P, K_TILES, LOWRANK], F16)
        stage = [[sb(f"stage{e}{s}", [P, BANK]) for s in range(2)] for e in range(2)]
        out = banks("out")
        glr_loaded = sem("glr_loaded")
        decay_loaded = sem("decay_loaded")
        ones_ready = sem("ones_ready")
        glr_cut = sem("glr_cut")
        glr_made = sem("glr_made")
        glr_kept = sem("glr_kept")
        hi_ready = [sem(f"w_hi_ready{s}") for s in range(2)]
        lo_ready = [sem(f"w_lo_ready{s}") for s in range(2)]
        out_ready = [sem(f"out_ready{e}") for e in range(2)]
        staged = [sem(f"staged{e}") for e in range(2)]
        stored = [[sem(f"stored{e}{s}") for s in range(2)] for e in range(2)]
        copied = sem("copied", start=0)
        ITERS = COLUMN_TILES // 2
        M = 2 * TOKEN_TILES
        PER = M // 2
        ROWS = [P] * (TOKEN_TILES - 1) + [TOKENS - (TOKEN_TILES - 1) * P]
        USES = [(PER + 1) // 2, PER // 2]
        nc.all_engine_barrier()
        block = ctx.enter_context(nc.Block())

        def shift(eng, cache, out, b):
            window = cache.shape[2]
            return eng.dma_start(out[0, bass.ds(b, 1), 0:window - DEC_SEQ].rearrange("b l k h d -> b l (k h d)"),
                                 cache[0, bass.ds(b, 1), DEC_SEQ:window].rearrange("b l k h d -> b l (k h d)"))

        @block.sync
        def _(sp):
            with nc.allow_non_contiguous_dma(reason="low-rank columns, once"):
                sp.dma_start(glr[:, :, :], w_view[:, :, W_LOWRANK:W_LOWRANK + LOWRANK]).then_inc(glr_loaded, 16)
            sp.dma_start(decay_w[0:LOWRANK, :], w_lr[0]).then_inc(decay_loaded, 16)
            sp.dma_start(decay_w[LOWRANK:LOWRANK + 1, :], b_lr).then_inc(decay_loaded, 16)

            def step(i, skip, last=False):
                for s in range(2):
                    if not last:
                        sp.wait_ge(lo_ready[s], START + i + 1)
                        sp.dma_start(raw[s][:, :, :], w_view[:, :, bass.ds((i + 1) * 2 * BANK + s * BANK + skip, BANK)]) \
                            .then_inc(raw_loaded[s], 16)
                    for t in range(TOKEN_TILES):
                        m = s * TOKEN_TILES + t
                        e, j = m % 2, m // 2
                        sp.wait_ge(staged[e], START + i * PER + j + 1)
                        sp.dma_start(U[t * P:t * P + ROWS[t], bass.ds(i * 2 * BANK + s * BANK, BANK)],
                                     stage[e][j % 2][:ROWS[t], :]).then_inc(stored[e][j % 2], 16)

            before = TILES_BEFORE_LOWRANK // 2 - 1
            with sp.Fori(0, before) as i:
                step(i, 0)
            with sp.Fori(before, ITERS - 1) as i:
                step(i, LOWRANK)
            step(ITERS - 1, LOWRANK, last=True)
            for e in range(2):
                for s in range(2):
                    sp.wait_ge(stored[e][s], START + ITERS * USES[s] * 16)
            sp.wait_ge(decay_loaded, START + 32)

        @block.gpsimd
        def _(pool):
            pool.memset(lowrank[:, :], 1.0).then_inc(ones_ready, 1)
            with pool.Fori(0, DEC_BATCH) as i:
                pool.wait_ge(raw_loaded[1], START + (i + 2) * 16)
                for cache, out in shift_cache:
                    shift(pool, cache, out, i).then_inc(copied, 16)
            pool.wait_ge(copied, DEC_BATCH * len(shift_cache) * 16)

        first = 0

        def was_last(i, s):
            return i * PER - PER + (TOKEN_TILES - 1) // 2 + 1 if s == 0 else i * PER

        def evacuate(eng, e, i, m, write):
            s, t = divmod(m, TOKEN_TILES)
            j = m // 2
            eng.wait_ge(out_ready[e], START + i * PER + j + 1)
            eng.wait_ge(stored[e][j % 2], START + (i * USES[j % 2] + j // 2) * 16)
            write(stage[e][j % 2][:ROWS[t], :], out[m % 8][:ROWS[t], :]).then_inc(staged[e], 1)

        @block.scalar
        def _(act):
            act.wait_ge(glr_loaded, START + 16)
            act.activation(glr_hi[:, :, :], glr[:, :, :], ACT.Copy, scale=W_SCALE).then_inc(glr_cut, 1)

            def cut(i, s):
                act.wait_ge(raw_loaded[s], START + (i + 1) * 16)
                if s == 1 or i is not first:
                    act.wait_ge(out_ready[s], START + was_last(i, s))
                act.activation(w_hi[s][:, :, :], raw[s][:, :, :], ACT.Copy, scale=W_SCALE).then_inc(hi_ready[s], 1)

            def step(i, last=False):
                for m in range(M):
                    if m == 0:
                        cut(i, 1)
                    if m == TOKEN_TILES and not last:
                        cut(i + 1, 0)
                    if m % 2 == 0:
                        evacuate(act, 0, i, m, lambda o, x: act.activation(o, x, ACT.Copy, scale=1.0 / W_SCALE))

            cut(first, 0)
            with act.Fori(0, ITERS - 1) as i:
                step(i)
            step(ITERS - 1, last=True)

        @block.vector
        def _(dve):
            dve.wait_ge(glr_loaded, START + 16)
            dve.wait_ge(glr_cut, START + 1)
            dve.scalar_tensor_tensor(out=glr_lo[:, :, :], in0=glr[:, :, :], scalar=W_SCALE, in1=glr_hi[:, :, :],
                                     op0=ALU.mult, op1=ALU.subtract).then_inc(glr_cut, 1)
            dve.wait_ge(ones_ready, START + 1)
            for c in range(5):
                n = min(BANK, TOKENS - c * BANK)
                dve.wait_ge(glr_made, START + c + 1)
                dve.tensor_scalar(lowrank[0:LOWRANK, c * BANK:c * BANK + n], out[c][0:LOWRANK, :n], 1.0 / W_SCALE, None,
                                  ALU.mult).then_inc(glr_kept, 1)

            def cut(i, s):
                dve.wait_ge(hi_ready[s], START + i + 1)
                if s == 1 or i is not first:
                    dve.wait_ge(out_ready[s], START + was_last(i, s))
                dve.scalar_tensor_tensor(out=w_lo[s][:, :, :], in0=raw[s][:, :, :], scalar=W_SCALE, in1=w_hi[s][:, :, :],
                                         op0=ALU.mult, op1=ALU.subtract).then_inc(lo_ready[s], 1)

            def step(i, last=False):
                for m in range(M):
                    if m == 0:
                        cut(i, 1)
                    if m == TOKEN_TILES and not last:
                        cut(i + 1, 0)
                    if m % 2 == 1:
                        evacuate(dve, 1, i, m, lambda o, x: dve.tensor_scalar(o, x, 1.0 / W_SCALE, None, ALU.mult))

            cut(first, 0)
            with dve.Fori(0, ITERS - 1) as i:
                step(i)
            step(ITERS - 1, last=True)

        @block.tensor
        def _(pe):
            pe.wait_ge(glr_cut, START + 2)
            for c in range(5):
                n = min(BANK, TOKENS - c * BANK)
                for k in range(K_TILES):
                    for a, b in ((glr_hi, xn_hi), (glr_hi, xn_lo), (glr_lo, xn_hi)):
                        last = pe.matmul(out[c][0:LOWRANK, :n], a[:, k, :], b[:, k, c * BANK:c * BANK + n],
                                         start=(k == 0 and a is glr_hi and b is xn_hi), stop=(k == K_TILES - 1 and a is glr_lo))
                last.then_inc(glr_made, 1)
            pe.wait_ge(glr_kept, START + 5)
            with pe.Fori(0, ITERS) as i:
                for s in range(2):
                    pe.wait_ge(hi_ready[s], START + i + 1)
                    pe.wait_ge(lo_ready[s], START + i + 1)
                    for t in range(TOKEN_TILES):
                        m = s * TOKEN_TILES + t
                        pe.wait_ge(staged[m % 2], START + (i * PER + (m - 8) // 2 + 1 if m >= 8 else i * PER))
                        rows, at = ROWS[t], t * P
                        for k in range(K_TILES):
                            passes = ((xn_hi, w_hi[s]), (xn_hi, w_lo[s]), (xn_lo, w_hi[s]))
                            for n, (a, b) in enumerate(passes):
                                last = pe.matmul(out[m % 8][:rows, :], a[:, k, at:at + rows], b[:, k, :],
                                                 start=(k == 0 and n == 0), stop=(k == K_TILES - 1 and n == 2))
                        last.then_inc(out_ready[m % 2], 1)


def prompt_windows(core, U, window_mask, identity, OG):
    nc = core.nc
    with ExitStack() as ctx:
        sb, sem, banks = core.bind(ctx)
        q = [sb(f"q{g}", [P, BLOCKS, HD]) for g in range(GROUPS)]
        k = [sb(f"k{g}", [P, BLOCKS, HD]) for g in range(GROUPS)]
        v = [sb(f"v{g}", [P, BLOCKS, HD]) for g in range(GROUPS)]
        qkT = [sb(f"qkT{g}", [P, BLOCKS, 2, P]) for g in range(GROUPS)]
        result = [sb(f"result{g}", [P, BLOCKS, HD + 2]) for g in range(GROUPS)]
        mask = sb("mask", [P, 2, P])
        score = [sb(f"score{s}", [P, 2, P]) for s in range(2)]
        prob = [sb(f"prob{s}", [P, 2, P]) for s in range(2)]
        probT = [sb(f"probT{s}", [P, 2, P]) for s in range(2)]
        top = [sb(f"top{s}", [P, 1]) for s in range(2)]
        bank = banks("win")
        mask_loaded = sem("mask_loaded")
        loaded = [sem(f"qkv_loaded{g}") for g in range(GROUPS)]
        stored = [sem(f"result_stored{g}") for g in range(GROUPS)]
        turned = sem("qk_turned")
        turned_kept = sem("qk_kept")
        scored = sem("scored")
        masked = sem("masked")
        top_ready = sem("top_ready")
        weighed = sem("weighed")
        prob_turned = sem("prob_turned")
        prob_kept = sem("prob_kept")
        summed = sem("summed")
        result_kept = sem("result_kept")
        STEPS = GROUPS * BLOCKS
        nc.all_engine_barrier()
        block = ctx.enter_context(nc.Block())

        def tokens(dram, g):
            dil = WINDOWS[g][1]
            return dram.rearrange("(n i r) c -> i n r c", i=SPAN, r=dil)

        def rings(tile, g):
            dil = WINDOWS[g][1]
            return tile.rearrange("p (n r) c -> p n r c", r=dil)

        def done(h, s, lag=0):
            return h * STEPS + max(s - lag + 1, 0)

        def first_key_block(s):
            g, b = divmod(s, BLOCKS)
            return 0 if b >= WINDOWS[g][1] else 1

        @block.sync
        def _(sp):
            sp.dma_start(mask[:, :, :], window_mask.rearrange("p (a j) -> p a j", a=2)).then_inc(mask_loaded, 16)

            def load(h, g):
                for tile, column in ((q[g], U_DQ), (k[g], U_DK), (v[g], U_DV)):
                    src = tokens(U[0:SEQ, bass.ds(h * HD + column + g * WIDTH, HD)], g)
                    dst = rings(tile[:, :, :], g)
                    for n in range(BLOCKS // WINDOWS[g][1]):
                        sp.dma_start(dst[:, n], src[:, n]).then_inc(loaded[g], 16)

            def step(h, last=False):
                for g in range(GROUPS):
                    sp.wait_ge(result_kept, START + done(h, (g + 1) * BLOCKS - 1))
                    dst = tokens(OG[0:SEQ, g, bass.ds(h * (HD + 2), HD + 2)], g)
                    src = rings(result[g][:, :, :], g)
                    for n in range(BLOCKS // WINDOWS[g][1]):
                        sp.dma_start(dst[:, n], src[:, n]).then_inc(stored[g], 16)
                    if not last:
                        load(h + 1, g)

            for g in range(GROUPS):
                load(0, g)
            with sp.Fori(0, HEADS - 1) as h:
                step(h)
            step(HEADS - 1, last=True)
            for g in range(GROUPS):
                sp.wait_ge(stored[g], START + HEADS * 16 * (BLOCKS // WINDOWS[g][1]))

        @block.tensor
        def _(pe):
            def turn(h, s):
                g, b = divmod(s, BLOCKS)
                if b == 0:
                    pe.wait_ge(loaded[g], START + (h + 1) * 3 * 16 * (BLOCKS // WINDOWS[g][1]))
                pe.wait_ge(turned_kept, START + done(h, s, 2))
                pe.transpose(bank[s % 2][:, 0:P], q[g][:, b, :], identity[:, :])
                pe.transpose(bank[s % 2][:, P:2 * P], k[g][:, b, :], identity[:, :]).then_inc(turned, 1)

            def scores(h, s):
                g, b = divmod(s, BLOCKS)
                dil, a = WINDOWS[g][1], first_key_block(s)
                pe.wait_ge(turned_kept, START + done(h, s))
                pe.wait_ge(masked, START + done(h, s, 2))
                keys = qkT[g][:, b - dil:b + 1:dil, 1, :] if a == 0 else qkT[g][:, b:b + 1, 1, :]
                out = bank[2 + s % 2][:, a * P:2 * P].rearrange("p (a j) -> p a j", j=P)
                pe.matmul(out, qkT[g][:, b, 0, :], keys, start=True, stop=True).then_inc(scored, 1)

            def turn_prob(h, s):
                pe.wait_ge(weighed, START + done(h, s))
                pe.wait_ge(prob_kept, START + done(h, s, 2))
                for a in range(first_key_block(s), 2):
                    last = pe.transpose(bank[4 + s % 2][:, a * P:(a + 1) * P], prob[s % 2][:, a, :], identity[:, :])
                last.then_inc(prob_turned, 1)

            def values(h, s):
                g, b = divmod(s, BLOCKS)
                dil, first = WINDOWS[g][1], first_key_block(s)
                pe.wait_ge(prob_kept, START + done(h, s))
                pe.wait_ge(result_kept, START + done(h, s, 2))
                for a in range(first, 2):
                    last = pe.matmul(bank[6 + s % 2][:, :HD], probT[s % 2][:, a, :], v[g][:, b - dil * (1 - a), :],
                                     start=(a == first), stop=(a == 1))
                last.then_inc(summed, 1)

            with pe.Fori(0, HEADS) as h:
                for s in range(STEPS + 4):
                    if s < STEPS:
                        turn(h, s)
                    if 1 <= s < STEPS + 1:
                        scores(h, s - 1)
                    if 3 <= s < STEPS + 3:
                        turn_prob(h, s - 3)
                    if s >= 4:
                        values(h, s - 4)

        @block.scalar
        def _(act):
            def keep_turned(h, s):
                g, b = divmod(s, BLOCKS)
                act.wait_ge(turned, START + done(h, s))
                act.wait_ge(scored, START + h * STEPS)
                act.activation(qkT[g][:, b, :, :], bank[s % 2][:, :2 * P].rearrange("p (a j) -> p a j", j=P),
                               ACT.Copy).then_inc(turned_kept, 1)

            def weigh(h, s):
                g, b = divmod(s, BLOCKS)
                a = first_key_block(s)
                if b == 0:
                    act.wait_ge(stored[g], START + h * 16 * (BLOCKS // WINDOWS[g][1]))
                act.wait_ge(top_ready, START + done(h, s))
                act.wait_ge(prob_turned, START + done(h, s, 2))
                act.activation(prob[s % 2][:, a:, :], score[s % 2][:, a:, :], ACT.Exp, scale=SCALE,
                               bias=result[g][:, b, HD:HD + 1], accum_out=result[g][:, b, HD + 1:HD + 2]).then_inc(weighed, 1)

            with act.Fori(0, HEADS) as h:
                for s in range(STEPS + 2):
                    if s < STEPS:
                        keep_turned(h, s)
                    if s >= 2:
                        weigh(h, s - 2)

        @block.vector
        def _(dve):
            dve.wait_ge(mask_loaded, START + 16)

            def mask_scores(h, s):
                g, b = divmod(s, BLOCKS)
                a = first_key_block(s)
                if b == 0:
                    dve.wait_ge(stored[g], START + h * 16 * (BLOCKS // WINDOWS[g][1]))
                dve.wait_ge(scored, START + done(h, s))
                dve.wait_ge(weighed, START + done(h, s, 2))
                apart(dve)
                dve.tensor_tensor_reduce(score[s % 2][:, a:, :],
                                         bank[2 + s % 2][:, a * P:2 * P].rearrange("p (a j) -> p a j", j=P),
                                         mask[:, a:, :], 1.0, MASKED, ALU.add, ALU.max, top[s % 2][:, :]).then_inc(masked, 1)
                dve.wait_ge(masked, START + done(h, s))
                dve.tensor_scalar(result[g][:, b, HD:HD + 1], top[s % 2][:, :], -SCALE, None,
                                  ALU.mult).then_inc(top_ready, 1)

            def keep_prob(h, s):
                dve.wait_ge(prob_turned, START + done(h, s))
                dve.wait_ge(summed, START + done(h, s, 2))
                a = first_key_block(s)
                dve.tensor_copy(probT[s % 2][:, a:, :],
                                bank[4 + s % 2][:, a * P:2 * P].rearrange("p (a j) -> p a j", j=P)).then_inc(prob_kept, 1)

            def keep_result(h, s):
                g, b = divmod(s, BLOCKS)
                dve.wait_ge(summed, START + done(h, s))
                dve.tensor_copy(result[g][:, b, :HD], bank[6 + s % 2][:, :HD]).then_inc(result_kept, 1)

            with dve.Fori(0, HEADS) as h:
                for s in range(STEPS + 4):
                    if 1 <= s < STEPS + 1:
                        mask_scores(h, s - 1)
                    if 3 <= s < STEPS + 3:
                        keep_prob(h, s - 3)
                    if s >= 4:
                        keep_result(h, s - 4)


def window_mask():
    i, j = np.arange(SPAN)[:, None], np.arange(SPAN)[None, :]
    before = np.where(j >= i, 0.0, MASKED)
    own = np.where(j <= i, 0.0, MASKED)
    return np.concatenate([before, own], axis=1).astype(np.float32)


def gla_recurrence(core, U, row0, C, chunks, state_in, state_out, lowrank, decay_w, causal, starts, identity, OA):
    nc = core.nc
    carried = state_in is None
    with ExitStack() as ctx:
        sb, sem, banks = core.bind(ctx, "prompt_" if carried else "sample_")
        HC = HEADS * C
        qk = [sb(f"qk{s}", [C, 2 * GLA_KEY]) for s in range(2)]
        v = [sb(f"v{s}", [C, GLA_VAL]) for s in range(2)]
        q_in = [sb(f"q_in{s}", [P, HEADS, C]) for s in range(2)]
        k_inv = [sb(f"k_inv{s}", [P, HEADS, C]) for s in range(2)]
        k_end = [sb(f"k_end{s}", [P, HEADS, C]) for s in range(2)]
        grow = [sb(f"grow{s}", [P, HEADS, C]) for s in range(2)]
        z_abs = sb("z_abs", [P, HC])
        z_exp = sb("z_exp", [P, HC])
        z_log = sb("z_log", [P, HC])
        log_a = sb("log_a", [P, HC])
        decay = sb("decay", [P, HEADS, C])
        to_end = sb("to_end", [P, HEADS, C])
        shrink = sb("shrink", [P, HEADS, C])
        end_decay = sb("end_decay", [P, HEADS, C])
        att = [sb(f"att{s}", [C, HEADS, C]) for s in range(2)]
        k_endT = [sb(f"k_endT{s}", [C, HEADS, P]) for s in range(2)]
        o = [sb(f"o{s}", [C, GLA_VAL]) for s in range(2)]
        state = [sb(f"state{s}", [P, HEADS, GLA_DV]) for s in range(2)]
        new_state = [state[1], state[0]] if carried else [sb(f"new_state{s}", [P, HEADS, GLA_DV]) for s in range(2)]
        causal_sb = sb("causal_sb", [C, HEADS, C])
        starts_sb = sb("starts_sb", [P, HC])
        bank = banks("gla")
        QK, Z, ATT, KE, O, S = bank[0], bank[1], bank[2], bank[3], bank[4:6], bank[6:8]
        const_loaded = sem("const_loaded")
        zeroed = sem("zeroed")
        qk_loaded = [sem(f"qk_loaded{s}") for s in range(2)]
        v_loaded = [sem(f"v_loaded{s}") for s in range(2)]
        state_loaded = [sem(f"state_loaded{s}") for s in range(2)]
        o_stored = [sem(f"o_stored{s}") for s in range(2)]
        state_stored = [sem(f"state_stored{s}") for s in range(2)]
        x_turned = sem("x_turned")
        z_abs_ready = sem("z_abs_ready")
        z_exp_ready = sem("z_exp_ready")
        z_log_ready = sem("z_log_ready")
        log_a_ready = sem("log_a_ready")
        decay_ready = sem("decay_ready")
        to_end_ready = sem("to_end_ready")
        exps_ready = sem("exps_ready")
        scaled = sem("scaled")
        att_made = sem("att_made")
        att_kept = sem("att_kept")
        k_end_kept = sem("k_end_kept")
        products = sem("state_products")
        state_ready = sem("state_ready")
        o_made = sem("o_made")
        o_kept = sem("o_kept")
        nc.all_engine_barrier()
        block = ctx.enter_context(nc.Block())

        def wait(eng, sem, n):
            if not isinstance(n, int) or n > 0:
                eng.wait_ge(sem, START + n)

        def pipeline(eng, prepare, attend, finish):
            prepare(0, 0)
            with eng.Fori(0, chunks // 2 - 1) as j:
                attend(j, 0)
                prepare(j, 1)
                finish(j, 0)
                attend(j, 1)
                prepare(j + 1, 0)
                finish(j, 1)
            j = chunks // 2 - 1
            attend(j, 0)
            prepare(j, 1)
            finish(j, 0)
            attend(j, 1)
            finish(j, 1)

        def rows(j, s):
            return bass.ds(j * (2 * C) + (row0 + s * C), C)

        def flat(tile):
            return tile[:, :, :].rearrange("p h c -> p (h c)")

        @block.sync
        def _(sp):
            sp.dma_start(causal_sb[:, :, :], causal.rearrange("p (h c) -> p h c", c=C)).then_inc(const_loaded, 16)
            sp.dma_start(starts_sb[:, :], starts).then_inc(const_loaded, 16)

            def load(j, s):
                c = 2 * j + s
                wait(sp, x_turned, c - 1)
                sp.dma_start(qk[s][:, :], U[rows(j, s), U_GQ:U_GQ + 2 * GLA_KEY]).then_inc(qk_loaded[s], 16)
                wait(sp, o_made, c - 1)
                sp.dma_start(v[s][:, :], U[rows(j, s), U_GV:U_GV + GLA_VAL]).then_inc(v_loaded[s], 16)
                if not carried:
                    wait(sp, state_ready, c - 1)
                    sp.dma_start(state[s][:, :, :], state_in[bass.ds(c, 1)].rearrange("b h d e -> d (b h) e")).then_inc(state_loaded[s], 16)

            def store(j, s):
                c = 2 * j + s
                sp.wait_ge(o_kept, START + c + 1)
                sp.dma_start(OA[rows(j, s), :], o[s][:, :]).then_inc(o_stored[s], 16)
                if not carried:
                    sp.wait_ge(state_ready, START + c + 1)
                    sp.dma_start(state_out[bass.ds(c, 1)].rearrange("b h d e -> d (b h) e"), new_state[s][:, :, :]).then_inc(state_stored[s], 16)

            load(0, 0)
            load(0, 1)
            last = chunks // 2 - 1
            with sp.Fori(0, last) as j:
                for s in range(2):
                    load(j + 1, s)
                    store(j, s)
            store(last, 0)
            store(last, 1)
            if carried:
                sp.wait_ge(state_ready, START + chunks)
                sp.dma_start(state_out[0].rearrange("h d e -> d h e"), state[chunks % 2][:, :, :]).then_inc(state_stored[0], 16)
                sp.wait_ge(state_stored[0], START + 16)
            for s in range(2):
                sp.wait_ge(o_stored[s], START + chunks // 2 * 16)
                if not carried:
                    sp.wait_ge(state_stored[s], START + chunks // 2 * 16)

        @block.tensor
        def _(pe):
            if carried:
                pe.wait_ge(zeroed, START + 3)

            def prepare(j, s):
                c = 2 * j + s
                pe.wait_ge(qk_loaded[s], START + 16 * j + 16)
                wait(pe, scaled, c)
                apart(pe)
                for n in range(2 * HEADS):
                    pe.transpose(QK[:, n * C:(n + 1) * C], qk[s][:, n * P:(n + 1) * P], identity[:C, :C])
                for h in range(HEADS):
                    last = pe.matmul(Z[:, h * C:(h + 1) * C], decay_w[:, h * P:(h + 1) * P], lowrank[:, rows(j, s)],
                                     start=True, stop=True)
                last.then_inc(x_turned, 1)

            def attend(j, s):
                c = 2 * j + s
                pe.wait_ge(scaled, START + c + 1)
                wait(pe, att_kept, c)
                wait(pe, k_end_kept, c)
                apart(pe)
                for h in range(HEADS):
                    pe.matmul(ATT[:C, h * C:(h + 1) * C], k_inv[s][:, h, :], q_in[s][:, h, :], start=True, stop=True)
                for h in range(HEADS):
                    last = pe.transpose(KE[:C, h * P:(h + 1) * P], k_end[s][:, h, :], identity[:, :])
                last.then_inc(att_made, 1)

            def finish(j, s):
                c = 2 * j + s
                pe.wait_ge(v_loaded[s], START + 16 * j + 16)
                pe.wait_ge(k_end_kept, START + c + 1)
                wait(pe, state_ready, c)
                apart(pe)
                for h in range(HEADS):
                    last = pe.matmul(S[h // 2][:, h % 2 * GLA_DV:(h % 2 + 1) * GLA_DV], k_endT[s][:, h, :],
                                     v[s][:, h * GLA_DV:(h + 1) * GLA_DV], start=True, stop=True)
                last.then_inc(products, 1)
                pe.wait_ge(att_kept, START + c + 1)
                wait(pe, o_kept, c)
                if not carried:
                    pe.wait_ge(state_loaded[s], START + 16 * j + 16)
                apart(pe)
                for h in range(HEADS):
                    out = O[h // 2][:C, h % 2 * GLA_DV:(h % 2 + 1) * GLA_DV]
                    pe.matmul(out, att[s][:, h, :], v[s][:, h * GLA_DV:(h + 1) * GLA_DV], start=True, stop=False)
                    last = pe.matmul(out, q_in[s][:, h, :], state[s][:, h, :], start=False, stop=True)
                last.then_inc(o_made, 1)

            pipeline(pe, prepare, attend, finish)

        @block.scalar
        def _(act):
            def prepare(j, s):
                c = 2 * j + s
                act.wait_ge(x_turned, START + c + 1)
                wait(act, z_exp_ready, c)
                act.activation(z_abs[:, :], Z[:, :HC], ACT.Abs).then_inc(z_abs_ready, 1)
                act.wait_ge(z_abs_ready, START + c + 1)
                wait(act, z_log_ready, c)
                act.activation(z_exp[:, :], z_abs[:, :], ACT.Exp, scale=-1.0).then_inc(z_exp_ready, 1)
                act.wait_ge(z_exp_ready, START + c + 1)
                wait(act, log_a_ready, c)
                act.activation(z_log[:, :], z_exp[:, :], ACT.Ln, bias=1.0).then_inc(z_log_ready, 1)
                act.wait_ge(decay_ready, START + c + 1)
                wait(act, scaled, c)
                wait(act, state_ready, c - 1)
                act.activation(grow[s][:, :, :], decay[:, :, :], ACT.Exp, scale=1.0 / GLA_TAU)
                act.activation(shrink[:, :, :], decay[:, :, :], ACT.Exp, scale=-1.0 / GLA_TAU)
                act.wait_ge(to_end_ready, START + c + 1)
                act.activation(end_decay[:, :, :], to_end[:, :, :], ACT.Exp, scale=1.0 / GLA_TAU).then_inc(exps_ready, 1)

            def attend(j, s):
                c = 2 * j + s
                act.wait_ge(att_made, START + c + 1)
                wait(act, products, 2 * j)
                act.activation(flat(k_endT[s]), KE[:C, :], ACT.Copy).then_inc(k_end_kept, 1)

            def finish(j, s):
                c = 2 * j + s
                act.wait_ge(o_made, START + c + 1)
                wait(act, o_stored[s], 16 * j)
                act.activation(o[s][:, 0:BANK], O[0][:C, :], ACT.Copy)
                act.activation(o[s][:, BANK:2 * BANK], O[1][:C, :], ACT.Copy).then_inc(o_kept, 1)

            pipeline(act, prepare, attend, finish)

        @block.vector
        def _(dve):
            for s in range(2):
                dve.memset(att[s][:, :, :], 0.0).then_inc(zeroed, 1)
            if carried:
                dve.memset(state[0][:, :, :], 0.0).then_inc(zeroed, 1)
            dve.wait_ge(zeroed, START + (3 if carried else 2))
            dve.wait_ge(const_loaded, START + 32)

            def prepare(j, s):
                c = 2 * j + s
                dve.wait_ge(z_log_ready, START + c + 1)
                dve.scalar_tensor_tensor(out=log_a[:, :], in0=Z[:, :HC], scalar=0.0, in1=z_log[:, :],
                                         op0=ALU.min, op1=ALU.subtract).then_inc(log_a_ready, 1)
                dve.wait_ge(log_a_ready, START + c + 1)
                wait(dve, exps_ready, c)
                dve.tensor_tensor_scan(flat(decay), starts_sb[:, :], log_a[:, :], 0.0,
                                       ALU.mult, ALU.add).then_inc(decay_ready, 1)
                dve.wait_ge(decay_ready, START + c + 1)
                dve.tensor_tensor(to_end[:, :, :], decay[:, :, C - 1:C].to_broadcast([P, HEADS, C]), decay[:, :, :],
                                  ALU.subtract).then_inc(to_end_ready, 1)
                dve.wait_ge(exps_ready, START + c + 1)
                wait(dve, o_made, c - 1)
                dve.scalar_tensor_tensor(out=flat(q_in[s]), in0=QK[:, 0:HC], scalar=GLA_DK ** -0.5, in1=flat(grow[s]),
                                         op0=ALU.mult, op1=ALU.mult)
                dve.tensor_tensor(flat(k_inv[s]), QK[:, HC:2 * HC], flat(shrink), ALU.mult)
                dve.tensor_tensor(flat(k_end[s]), QK[:, HC:2 * HC], flat(end_decay), ALU.mult).then_inc(scaled, 1)

            def attend(j, s):
                c = 2 * j + s
                dve.wait_ge(att_made, START + c + 1)
                wait(dve, o_made, 2 * j)
                apart(dve)
                dve.copy_predicated(flat(att[s]), flat(causal_sb).bitcast(mybir.dt.int32),
                                    ATT[:C, :HC]).then_inc(att_kept, 1)

            def finish(j, s):
                c = 2 * j + s
                dve.wait_ge(products, START + c + 1)
                if carried:
                    wait(dve, o_made, c)
                else:
                    dve.wait_ge(state_loaded[s], START + 16 * j + 16)
                    wait(dve, state_stored[s], 16 * j)
                for h in range(HEADS):
                    last = dve.scalar_tensor_tensor(out=new_state[s][:, h, :], in0=state[s][:, h, :],
                                                    scalar=grow[s][:, h, C - 1:C],
                                                    in1=S[h // 2][:, h % 2 * GLA_DV:(h % 2 + 1) * GLA_DV],
                                                    op0=ALU.mult, op1=ALU.add)
                last.then_inc(state_ready, 1)

            pipeline(dve, prepare, attend, finish)


def causal_mask(C):
    one = (np.arange(C)[:, None] <= np.arange(C)[None, :]).astype(np.float32)
    return np.tile(one, (1, HEADS))


def scan_starts(C):
    row = np.ones((HEADS, C), np.float32)
    row[:, 0] = 0.0
    return np.broadcast_to(row.reshape(1, -1), (P, HEADS * C)).copy()


CACHE_BLOCKS = [(g, r) for g, (_, dil) in enumerate(WINDOWS) for r in range(min(dil, DEC_SEQ))]
N_CACHE = len(CACHE_BLOCKS)
N_BLOCKS = N_CACHE + 1
NEW_KEYS = GROUPS * DEC_SEQ
KEYS = N_CACHE * P + NEW_KEYS
QUAD = 32
PER_BANK = BANK // P
SCORE_BANKS = -(-N_BLOCKS // PER_BANK)


def sample_mask():
    mask = np.full((P, KEYS), MASKED, np.float32)
    for t in range(DEC_SEQ):
        one = np.full(KEYS, MASKED, np.float32)
        for n, (g, r) in enumerate(CACHE_BLOCKS):
            window, dil = WINDOWS[g]
            back = window + t - (np.arange(P) * dil + r)
            one[n * P:(n + 1) * P][(back % dil == 0) & (back <= window)] = 0.0
        for g, (window, dil) in enumerate(WINDOWS):
            back = t - np.arange(DEC_SEQ)
            one[N_CACHE * P + g * DEC_SEQ:][:DEC_SEQ][(back >= 0) & (back % dil == 0)] = 0.0
        mask[t::QUAD] = one
    return mask


def sample_windows(core, U, caches, mask_in, identity, OG):
    nc = core.nc
    with ExitStack() as ctx:
        sb, sem, banks = core.bind(ctx, "sw_")
        kv = [[sb(f"kv{s}_{n}", [P, 2 * WIDTH]) for n in range(N_CACHE)] for s in range(2)]
        kv_new = [sb(f"kv_new{s}", [NEW_KEYS, 2 * WIDTH]) for s in range(2)]
        q = [sb(f"q{s}", [DEC_SEQ, GROUPS * WIDTH]) for s in range(2)]
        qT = [sb(f"qT{s}", [P, GROUPS * HEADS, QUAD]) for s in range(2)]
        kT = [sb(f"kT{s}", [P, HEADS, P]) for s in range(2)]
        prob = [sb(f"prob{s}", [P, KEYS]) for s in range(2)]
        probT = [sb(f"probT{s}", [P, N_BLOCKS, P]) for s in range(2)]
        mask = sb("mask", [P, KEYS])
        tops = [sb(f"tops{s}", [P, SCORE_BANKS]) for s in range(2)]
        top = [sb(f"top{s}", [P, 1]) for s in range(2)]
        result = [sb(f"result{s}", [P, HD + 2]) for s in range(2)]
        empty = sb("empty", [SAMPLES, (GROUPS - 1) * HEADS, HD + 2])
        bank = banks("sw")
        KT, SC, PT, Q, O = bank[0:2], bank[2:4], bank[4:6], bank[6], bank[7]
        mask_loaded = sem("mask_loaded")
        zeroed = sem("zeroed")
        empty_stored = sem("empty_stored")
        q_loaded = [sem(f"q_loaded{s}") for s in range(2)]
        kv_loaded = [[sem(f"kv_loaded{s}_{n}") for n in range(N_BLOCKS)] for s in range(2)]
        q_turned = sem("q_turned")
        q_kept = sem("q_kept")
        k_turned = sem("k_turned")
        k_kept = sem("k_kept")
        block_scored = sem("block_scored")
        masked = sem("masked")
        topped = sem("topped")
        top_ready = sem("top_ready")
        weighed = sem("weighed")
        p_turned = sem("p_turned")
        p_kept = sem("p_kept")
        summed = sem("summed")
        o_kept = sem("o_kept")
        o_stored = [sem(f"o_stored{s}") for s in range(2)]
        PAIRS = DEC_BATCH // 2
        nc.all_engine_barrier()
        block = ctx.enter_context(nc.Block())

        def widths(m):
            blocks = range(m * PER_BANK, min((m + 1) * PER_BANK, N_BLOCKS))
            return blocks, min(BANK, KEYS - m * BANK)

        @block.sync
        def _(sp):
            sp.dma_start(mask[:, :], mask_in).then_inc(mask_loaded, 16)
            sp.wait_ge(zeroed, START + 4)
            with nc.allow_non_contiguous_dma(reason="once"):
                sp.dma_start(OG[SEQ:TOKENS, 1:GROUPS, :], empty[:, :, :].rearrange("t (g h) c -> t g (h c)", h=HEADS)) \
                    .then_inc(empty_stored, 16)

            def load(j, s):
                c = 2 * j + s
                rows = bass.ds(c * DEC_SEQ + SEQ, DEC_SEQ)
                sp.dma_start(q[s][:, :], U[rows, U_DQ:U_DQ + GROUPS * WIDTH]).then_inc(q_loaded[s], 16)
                for n, (g, r) in enumerate(CACHE_BLOCKS):
                    window, dil = WINDOWS[g]
                    src = caches[g][0, bass.ds(c, 1)].rearrange("b (l r) k h d -> r l (b k h d)", r=dil)
                    sp.dma_start(kv[s][n][:, :], src[r]).then_inc(kv_loaded[s][n], 16)
                for g in range(GROUPS):
                    for part, column in ((0, U_DK), (1, U_DV)):
                        sp.dma_start(kv_new[s][g * DEC_SEQ:(g + 1) * DEC_SEQ, part * WIDTH:(part + 1) * WIDTH],
                                     U[rows, column + g * WIDTH:column + (g + 1) * WIDTH]).then_inc(kv_loaded[s][N_CACHE], 16)

            def store(j, s):
                c = 2 * j + s
                sp.wait_ge(o_kept, START + c + 1)
                for h in range(HEADS):
                    rows = bass.ds(c * DEC_SEQ + SEQ, DEC_SEQ)
                    sp.dma_start(OG[rows, 0, h * (HD + 2):(h + 1) * (HD + 2)], result[s][h * QUAD:h * QUAD + DEC_SEQ, :]).then_inc(o_stored[s], 16)

            def step(j, last=False):
                for s in range(2):
                    sp.wait_ge(summed, START + 2 * j + s + 1)
                    if not last:
                        load(j + 1, s)
                for s in range(2):
                    store(j, s)

            load(0, 0)
            load(0, 1)
            with sp.Fori(0, PAIRS - 1) as j:
                step(j)
            step(PAIRS - 1, last=True)
            for s in range(2):
                sp.wait_ge(o_stored[s], START + PAIRS * HEADS * 16)
            sp.wait_ge(empty_stored, START + 16)

        @block.gpsimd
        def _(pool):
            for s in range(2):
                pool.memset(qT[s][:, :, :], 0.0).then_inc(zeroed, 1)
            pool.memset(empty[:, :, :], 0.0).then_inc(zeroed, 1)
            pool.wait_ge(zeroed, START + 3)
            pool.memset(empty[:, :, HD:HD + 1], -MASKED).then_inc(zeroed, 1)

        @block.tensor
        def _(pe):
            pe.wait_ge(zeroed, START + 4)

            def query(j, s):
                c = 2 * j + s
                pe.wait_ge(q_loaded[s], START + 16 * j + 16)
                pe.wait_ge(q_kept, START + c)
                apart(pe)
                for n in range(GROUPS * HEADS):
                    last = pe.transpose(Q[:, n * DEC_SEQ:(n + 1) * DEC_SEQ], q[s][:, n * P:(n + 1) * P], identity[:DEC_SEQ, :DEC_SEQ])
                last.then_inc(q_turned, 1)

            def turn_keys(j, s, n):
                c = 2 * j + s
                pe.wait_ge(kv_loaded[s][n], START + ((16 * j + 16) * (1 if n < N_CACHE else 2 * GROUPS)))
                pe.wait_ge(k_kept, START + c * N_BLOCKS + max(n - 1, 0))
                keys, src = (P, kv[s][n]) if n < N_CACHE else (NEW_KEYS, kv_new[s])
                apart(pe)
                for h in range(HEADS):
                    last = pe.transpose(KT[n % 2][:, h * P:h * P + keys], src[:, h * P:(h + 1) * P], identity[:keys, :keys])
                last.then_inc(k_turned, 1)

            def score(j, s, n):
                c = 2 * j + s
                m = n // PER_BANK
                pe.wait_ge(k_kept, START + c * N_BLOCKS + n + 1)
                if n == 0:
                    pe.wait_ge(q_kept, START + c + 1)
                if n % PER_BANK == 0:
                    pe.wait_ge(masked, START + c * SCORE_BANKS + max(m - 1, 0))
                for h in range(HEADS):
                    at = n % PER_BANK * P
                    out = SC[m % 2][h * QUAD:(h + 1) * QUAD, :]
                    if n < N_CACHE:
                        g = CACHE_BLOCKS[n][0]
                        last = pe.matmul(out[:, at:at + P], qT[s][:, g * HEADS + h, :], kT[n % 2][:, h, :], start=True, stop=True)
                    else:
                        for g in range(GROUPS):
                            last = pe.matmul(out[:, at + g * DEC_SEQ:at + (g + 1) * DEC_SEQ], qT[s][:, g * HEADS + h, :],
                                             kT[n % 2][:, h, g * DEC_SEQ:(g + 1) * DEC_SEQ], start=True, stop=True)
                last.then_inc(block_scored, 1)

            def turn_prob(j, s, m):
                c = 2 * j + s
                pe.wait_ge(weighed, START + c + 1)
                pe.wait_ge(p_kept, START + c * SCORE_BANKS + max(m - 1, 0))
                blocks, _ = widths(m)
                for n in blocks:
                    keys = P if n < N_CACHE else NEW_KEYS
                    last = pe.transpose(PT[m % 2][:keys, n % PER_BANK * P:(n % PER_BANK + 1) * P],
                                        prob[s][:, n * P:n * P + keys], identity[:, :])
                last.then_inc(p_turned, 1)

            def values(j, s):
                c = 2 * j + s
                pe.wait_ge(p_kept, START + (c + 1) * SCORE_BANKS)
                pe.wait_ge(o_kept, START + c)
                for n in range(N_BLOCKS):
                    keys, src = (P, kv[s][n]) if n < N_CACHE else (NEW_KEYS, kv_new[s])
                    for h in range(HEADS):
                        last = pe.matmul(O[h * QUAD:(h + 1) * QUAD, :HD], probT[s][:keys, n, h * QUAD:(h + 1) * QUAD],
                                         src[:, WIDTH + h * HD:WIDTH + (h + 1) * HD], start=(n == 0), stop=(n == N_BLOCKS - 1))
                last.then_inc(summed, 1)

            with pe.Fori(0, PAIRS) as j:
                for s in range(2):
                    query(j, s)
                    for n in range(N_BLOCKS + 1):
                        if n < N_BLOCKS:
                            turn_keys(j, s, n)
                        if n:
                            score(j, s, n - 1)
                for s in range(2):
                    for m in range(SCORE_BANKS):
                        turn_prob(j, s, m)
                    values(j, s)

        @block.scalar
        def _(act):
            def keep_keys(j, s, n):
                c = 2 * j + s
                act.wait_ge(k_turned, START + c * N_BLOCKS + n + 1)
                act.wait_ge(block_scored, START + c * N_BLOCKS + max(n - 1, 0))
                keys = P if n < N_CACHE else NEW_KEYS
                act.activation(kT[n % 2][:, :, :keys], KT[n % 2][:, :].rearrange("p (h k) -> p h k", h=HEADS)[:, :, :keys],
                               ACT.Copy).then_inc(k_kept, 1)

            def weigh(j, s):
                c = 2 * j + s
                act.wait_ge(top_ready, START + c + 1)
                act.activation(prob[s][:, :], prob[s][:, :], ACT.Exp, scale=SCALE, bias=result[s][:, HD:HD + 1],
                               accum_out=result[s][:, HD + 1:HD + 2]).then_inc(weighed, 1)

            with act.Fori(0, PAIRS) as j:
                for s in range(2):
                    for n in range(N_BLOCKS):
                        keep_keys(j, s, n)
                    weigh(j, s)

        @block.vector
        def _(dve):
            dve.wait_ge(mask_loaded, START + 16)
            dve.wait_ge(zeroed, START + 4)

            def keep_query(j, s):
                c = 2 * j + s
                dve.wait_ge(q_turned, START + c + 1)
                dve.tensor_copy(qT[s][:, :, :DEC_SEQ], Q[:, :GROUPS * HEADS * DEC_SEQ].rearrange("p (n t) -> p n t", t=DEC_SEQ)) \
                   .then_inc(q_kept, 1)

            def mask_scores(j, s, m):
                c = 2 * j + s
                blocks, w = widths(m)
                dve.wait_ge(block_scored, START + c * N_BLOCKS + blocks[-1] + 1)
                if m == 0:
                    dve.wait_ge(o_stored[s], START + j * HEADS * 16)
                    dve.wait_ge(p_turned, START + 2 * j * SCORE_BANKS)
                apart(dve)
                dve.tensor_tensor_reduce(prob[s][:, m * BANK:m * BANK + w], SC[m % 2][:, :w], mask[:, m * BANK:m * BANK + w],
                                         1.0, MASKED, ALU.add, ALU.max, tops[s][:, m:m + 1]).then_inc(masked, 1)

            def find_top(j, s):
                c = 2 * j + s
                dve.wait_ge(masked, START + (c + 1) * SCORE_BANKS)
                dve.tensor_reduce(top[s][:, :], tops[s][:, :], AX_X, ALU.max).then_inc(topped, 1)
                dve.wait_ge(topped, START + c + 1)
                dve.tensor_scalar(result[s][:, HD:HD + 1], top[s][:, :], -SCALE, None, ALU.mult).then_inc(top_ready, 1)

            def keep_prob(j, s, m):
                c = 2 * j + s
                dve.wait_ge(p_turned, START + c * SCORE_BANKS + m + 1)
                dve.wait_ge(summed, START + 2 * j)
                blocks, _ = widths(m)
                full = [n for n in blocks if n < N_CACHE]
                src = PT[m % 2][:, :].rearrange("p (n k) -> p n k", k=P)
                last = dve.tensor_copy(probT[s][:, full[0]:full[-1] + 1, :], src[:, :len(full), :])
                if len(full) < len(blocks):
                    last = dve.tensor_copy(probT[s][:NEW_KEYS, N_CACHE, :], src[:NEW_KEYS, len(full), :])
                last.then_inc(p_kept, 1)

            def keep_output(j, s):
                c = 2 * j + s
                dve.wait_ge(summed, START + c + 1)
                dve.tensor_copy(result[s][:, :HD], O[:, :HD]).then_inc(o_kept, 1)

            with dve.Fori(0, PAIRS) as j:
                for s in range(2):
                    keep_query(j, s)
                    for m in range(SCORE_BANKS):
                        mask_scores(j, s, m)
                    find_top(j, s)
                for s in range(2):
                    for m in range(SCORE_BANKS):
                        keep_prob(j, s, m)
                    keep_output(j, s)


def mix_outputs(core, U, OG, OA, x_prompt, x_sample, p_prompt, p_sample, weights, g_gla, g_post, identity, y_prompt, y_sample):
    nc = core.nc
    with ExitStack() as ctx:
        sb, sem, banks = core.bind(ctx, "mix_")
        N_Z = (GLA_VAL + WIDTH) // P
        first, n_slices = {}, 0
        for name, w in weights:
            first[name] = n_slices
            n_slices += w.shape[1] // P
        w_hi = sb("w_hi", [P, n_slices, D_MODEL], F16)
        w_lo = sb("w_lo", [P, n_slices, D_MODEL], F16)
        og = [sb(f"og{s}", [P, GROUPS * HEADS, HD + 2]) for s in range(2)]
        oa = [sb(f"oa{s}", [P, HEADS, GLA_DV]) for s in range(2)]
        gg = [sb(f"gg{s}", [P, HEADS, GLA_DV]) for s in range(2)]
        dg = [sb(f"dg{s}", [P, HEADS, HD]) for s in range(2)]
        ga = [sb(f"ga{s}", [P, D_MODEL]) for s in range(2)]
        gb = [sb(f"gb{s}", [P, D_MODEL]) for s in range(2)]
        x = [sb(f"x{s}", [P, D_MODEL]) for s in range(2)]
        pe_in = [sb(f"pe{s}", [P, PLE]) for s in range(2)]
        zT = [[sb(f"zT{s}{part}", [P, N_Z, P], F16) for part in "hl"] for s in range(2)]
        mT = [[sb(f"mT{s}{part}", [P, K_TILES, P], F16) for part in "hl"] for s in range(2)]
        peT = [[sb(f"peT{s}{part}", [P, PLE // P, P], F16) for part in "hl"] for s in range(2)]
        g_post_sb = sb("g_post_sb", [P, D_MODEL])
        g_gla_sb = sb("g_gla_sb", [P, K_TILES])
        junk = sb("junk", [P, BANK], F16)
        power = sb("power", [P, HEADS])
        least = [sb(f"least{s}", [P, HEADS]) for s in range(2)]
        share = [sb(f"share{s}", [P, GROUPS, HEADS]) for s in range(2)]
        shareL = [sb(f"shareL{s}", [P, GROUPS, HEADS]) for s in range(2)]
        total = [sb(f"total{s}", [P, HEADS]) for s in range(2)]
        mean_a = [sb(f"mean_a{s}", [P, HEADS]) for s in range(2)]
        rstd_a = [sb(f"rstd_a{s}", [P, HEADS]) for s in range(2)]
        mean_m = [sb(f"mean_m{s}", [P, 2]) for s in range(2)]
        rstd_m = [sb(f"rstd_m{s}", [P, 1]) for s in range(2)]
        bank = banks("mix")
        T, Y, W = bank[0:2], bank[2:6], bank[6:8]
        OUT, GATE, PROJ = [W, Y[0:2]], [Y[2:4], Y[0:2]], [W, Y[2:4]]
        RAW = [ga[0], gb[0], ga[1], gb[1]]

        g_loaded = sem("g_loaded")
        g_scaled = sem("g_scaled")
        raw_loaded = [sem(f"raw_loaded{r}") for r in range(4)]
        w_hi_ready = sem("w_hi_ready")
        w_lo_ready = sem("w_lo_ready")
        power_ready = sem("power_ready")
        early_loaded = [sem(f"early_loaded{s}") for s in range(2)]
        late_loaded = [sem(f"late_loaded{s}") for s in range(2)]
        y_stored = [sem(f"y_stored{s}") for s in range(2)]

        def per_slot(name):
            return [sem(f"{name}{s}") for s in range(2)]

        dve_step = sem("dve_step")
        pool_step = sem("pool_step")
        share_asked = per_slot("share_asked")
        share_made = per_slot("share_made")
        mean_a_ready = per_slot("mean_a_ready")
        rstd_a_ready = per_slot("rstd_a_ready")
        silu_ready = per_slot("silu_ready")
        gates_ready = per_slot("gates_ready")
        z_ready = per_slot("z_ready")
        y_made = per_slot("y_made")
        merged = per_slot("merged")
        out_made = per_slot("out_made")
        mean_m_ready = per_slot("mean_m_ready")
        rstd_m_ready = per_slot("rstd_m_ready")
        h_ready = per_slot("h_ready")
        gate_made = per_slot("gate_made")
        gate_ready = per_slot("gate_ready")
        proj_made = per_slot("proj_made")
        y_ready = per_slot("y_ready")
        turned = sem("turned")
        hi_ready = sem("hi_ready")
        lo_ready = sem("lo_ready")
        PAIRS = SEQ // P // 2
        Z_CHUNKS, M_CHUNKS = 4, 2
        PAIR_CHUNKS = 2 * (Z_CHUNKS + 2 * M_CHUNKS)
        nc.all_engine_barrier()
        block = ctx.enter_context(nc.Block())

        def iterations(eng, step):
            with eng.Fori(0, PAIRS) as j:
                step(j, (0, 1), P)
            step(PAIRS, (0,), SAMPLES)

        def chunk(j, slots, stage, s, n):
            per = (Z_CHUNKS, M_CHUNKS, M_CHUNKS)
            at = sum(per[:stage]) * len(slots) + s * per[stage] + n
            return j * PAIR_CHUNKS + at, at % 2

        def tile_rows(tile):
            return bass.ds(tile * P, P)

        @block.sync
        def _(sp):
            with nc.allow_non_contiguous_dma(reason="gains, once"):
                sp.dma_start(g_gla_sb[:, :], g_gla[0].rearrange("(k p) -> p k", p=P)).then_inc(g_loaded, 16)
                sp.dma_start(g_post_sb[:, :], g_post.to_broadcast([P, D_MODEL])).then_inc(g_loaded, 16)
            n = 0
            for name, w in weights:
                for k in range(w.shape[1] // P):
                    if n >= 4:
                        sp.wait_ge(w_lo_ready, START + n - 3)
                    sp.dma_start(RAW[n % 4][:, :], w[0, k * P:(k + 1) * P, :]).then_inc(raw_loaded[n % 4], 16)
                    n += 1

            def early(tile, s, rows):
                at = tile_rows(tile) if rows == P else slice(SEQ, TOKENS)
                sp.dma_start(og[s][:rows, :, :], OG[at].rearrange("t g (h c) -> t (g h) c", h=HEADS)).then_inc(early_loaded[s], 16)
                sp.dma_start(oa[s][:rows, :, :], OA[at].rearrange("t (h c) -> t h c", h=HEADS)).then_inc(early_loaded[s], 16)
                sp.dma_start(gg[s][:rows, :, :], U[at, U_GG:U_GG + GLA_VAL].rearrange("t (h c) -> t h c", h=HEADS)).then_inc(early_loaded[s], 16)
                sp.dma_start(dg[s][:rows, :, :], U[at, U_DG:U_DG + WIDTH].rearrange("t (h c) -> t h c", h=HEADS)).then_inc(early_loaded[s], 16)
                src = p_prompt[0, 0, at, :] if rows == P else p_sample[0].rearrange("b t d -> (b t) d")
                sp.dma_start(pe_in[s][:rows, :], src).then_inc(early_loaded[s], 16)

            def late(tile, s, rows):
                at = tile_rows(tile) if rows == P else slice(SEQ, TOKENS)
                sp.dma_start(ga[s][:rows, :], U[at, U_GA:U_GA + D_MODEL]).then_inc(late_loaded[s], 16)
                sp.dma_start(gb[s][:rows, :], U[at, U_GB:U_GB + D_MODEL]).then_inc(late_loaded[s], 16)
                src = x_prompt[0, at, :] if rows == P else x_sample.rearrange("b t d -> (b t) d")
                sp.dma_start(x[s][:rows, :], src).then_inc(late_loaded[s], 16)

            def step(j, slots, after):
                for s, rows in after.items():
                    sp.wait_ge(turned, START + chunk(j, slots, 0, s, Z_CHUNKS - 1)[0] + 1)
                    early((j + 1) * 2 + s, s, rows)
                for s in slots:
                    sp.wait_ge(y_ready[s], START + j + 1)
                    if isinstance(j, int) and j == PAIRS:
                        sp.dma_start(y_sample.rearrange("b t d -> (b t) d"), x[s][:SAMPLES, :]).then_inc(y_stored[s], 16)
                    else:
                        sp.dma_start(y_prompt[0, tile_rows(2 * j + s), :], x[s][:, :]).then_inc(y_stored[s], 16)
                    if s in after:
                        sp.wait_ge(y_stored[s], START + (j + 1) * 16)
                        late((j + 1) * 2 + s, s, after[s])

            for s in range(2):
                early(s, s, P)
            sp.wait_ge(w_lo_ready, START + n_slices)
            for s in range(2):
                late(s, s, P)
            with sp.Fori(0, PAIRS - 1) as j:
                step(j, (0, 1), {0: P, 1: P})
            step(PAIRS - 1, (0, 1), {0: SAMPLES})
            step(PAIRS, (0,), {})
            sp.wait_ge(y_stored[0], START + (PAIRS + 1) * 16)
            sp.wait_ge(y_stored[1], START + PAIRS * 16)

        @block.gpsimd
        def _(pool):
            pool.memset(power[:, :], -0.5).then_inc(power_ready, 1)
            pool.wait_ge(power_ready, START + 1)

            def step(j, slots, rows):
                done = [0]

                def link(instruction):
                    done[0] += 1
                    instruction.then_inc(pool_step, 1)
                    pool.wait_ge(pool_step, START + j * 8 + done[0])

                for s in slots:
                    pool.wait_ge(mean_a_ready[s], START + (j + 1) * HEADS)
                    apart(pool)
                    link(pool.tensor_scalar(mean_a[s][:rows, :], mean_a[s][:rows, :], NORM_EPS, None, ALU.add))
                    pool.wait_ge(z_ready[s], START + j)
                    pool.tensor_tensor(rstd_a[s][:rows, :], mean_a[s][:rows, :], power[:rows, :], ALU.pow).then_inc(rstd_a_ready[s], 1)
                for s in slots:
                    pool.wait_ge(mean_m_ready[s], START + (j + 1) * 2)
                    link(pool.tensor_tensor(mean_m[s][:rows, 0:1], mean_m[s][:rows, 0:1], mean_m[s][:rows, 1:2], ALU.add))
                    apart(pool)
                    link(pool.tensor_scalar(mean_m[s][:rows, 0:1], mean_m[s][:rows, 0:1], NORM_EPS, None, ALU.add))
                    pool.wait_ge(h_ready[s], START + j)
                    link(pool.tensor_tensor(rstd_m[s][:rows, :], mean_m[s][:rows, 0:1], power[:rows, 0:1], ALU.pow))
                    apart(pool)
                    pool.tensor_scalar(rstd_m[s][:rows, :], rstd_m[s][:rows, :], 1.0 / W_SCALE, None, ALU.mult).then_inc(rstd_m_ready[s], 1)

            iterations(pool, step)

        @block.scalar
        def _(act):
            act.wait_ge(g_scaled, START + 1)
            for n in range(n_slices):
                act.wait_ge(raw_loaded[n % 4], START + 16 * (n // 4 + 1))
                gla = n < GLA_VAL // P
                act.activation(w_hi[:, n, :], RAW[n % 4][:, :], ACT.Copy,
                               scale=g_gla_sb[:, n:n + 1] if gla else W_SCALE).then_inc(w_hi_ready, 1)

            def hi(j, slots, stage, s, n, out, rows):
                c, b = chunk(j, slots, stage, s, n)
                act.wait_ge(turned, START + c + 1)
                blocks = out.shape[1]
                act.activation(out, T[b][:, :blocks * P].rearrange("p (n t) -> p n t", t=P)[:, :, :rows], ACT.Copy).then_inc(hi_ready, 1)

            def step(j, slots, rows):
                for s in slots:
                    act.wait_ge(share_asked[s], START + j + 1)
                    act.activation(share[s][:rows, :, :], share[s][:rows, :, :], ACT.Exp).then_inc(share_made[s], 1)
                for s in slots:
                    act.wait_ge(early_loaded[s], START + (j + 1) * 5 * 16)
                    act.wait_ge(rstd_a_ready[s], START + j)
                    for h in range(HEADS):
                        act.activation(junk[:rows, :GLA_DV], oa[s][:rows, h, :], ACT.Square, scale=GLA_DV ** -0.5,
                                       accum_out=mean_a[s][:rows, h:h + 1]).then_inc(mean_a_ready[s], 1)
                        act.wait_ge(mean_a_ready[s], START + j * HEADS + h + 1)
                for s in slots:
                    act.activation(gg[s][:rows, :, :], gg[s][:rows, :, :], ACT.Silu).then_inc(silu_ready[s], 1)
                    act.activation(dg[s][:rows, :, :], dg[s][:rows, :, :], ACT.Silu).then_inc(silu_ready[s], 1)
                for s in slots:
                    act.wait_ge(late_loaded[s], START + (j + 1) * 3 * 16)
                    act.activation(ga[s][:rows, :], ga[s][:rows, :], ACT.Sigmoid).then_inc(gates_ready[s], 1)
                    act.activation(gb[s][:rows, :], gb[s][:rows, :], ACT.Sigmoid).then_inc(gates_ready[s], 1)
                for s in slots:
                    act.wait_ge(y_made[s], START + j)
                    act.wait_ge(proj_made[s], START + j)
                    for n in range(3):
                        hi(j, slots, 0, s, n, zT[s][0][:, 4 * n:4 * n + 4, :rows], rows)
                    hi(j, slots, 0, s, 3, peT[s][0][:, :, :rows], rows)
                for s in slots:
                    act.wait_ge(gate_made[s], START + j)
                    for n in range(2):
                        hi(j, slots, 1, s, n, mT[s][0][:, 4 * n:4 * n + 4, :rows], rows)
                for s in slots:
                    act.wait_ge(out_made[s], START + j + 1)
                    for n in range(2):
                        act.activation(junk[:rows, :], OUT[s][n][:rows, :], ACT.Square, scale=D_MODEL ** -0.5 / W_SCALE,
                                       accum_out=mean_m[s][:rows, n:n + 1]).then_inc(mean_m_ready[s], 1)
                        act.wait_ge(mean_m_ready[s], START + j * 2 + n + 1)
                for s in slots:
                    for n in range(2):
                        hi(j, slots, 2, s, n, mT[s][0][:, 4 * n:4 * n + 4, :rows], rows)
                for s in slots:
                    act.wait_ge(gate_made[s], START + j + 1)
                    act.wait_ge(h_ready[s], START + j + 1)
                    for n in range(2):
                        act.activation(gb[s][:rows, n * BANK:(n + 1) * BANK], GATE[s][n][:rows, :], ACT.Sigmoid,
                                       scale=1.0 / W_SCALE).then_inc(gate_ready[s], 1)

            iterations(act, step)

        @block.vector
        def _(dve):
            dve.wait_ge(g_loaded, START + 32)
            dve.tensor_scalar(g_gla_sb[:, :], g_gla_sb[:, :], W_SCALE, None, ALU.mult).then_inc(g_scaled, 1)
            dve.wait_ge(g_scaled, START + 1)
            for n in range(n_slices):
                dve.wait_ge(w_hi_ready, START + n + 1)
                gla = n < GLA_VAL // P
                dve.scalar_tensor_tensor(out=w_lo[:, n, :], in0=RAW[n % 4][:, :], scalar=g_gla_sb[:, n:n + 1] if gla else W_SCALE,
                                         in1=w_hi[:, n, :], op0=ALU.mult, op1=ALU.subtract).then_inc(w_lo_ready, 1)

            def lo(j, slots, stage, s, n, out, part, rows):
                c, b = chunk(j, slots, stage, s, n)
                dve.wait_ge(hi_ready, START + c + 1)
                blocks = out.shape[1]
                dve.tensor_tensor(out, T[b][:, :blocks * P].rearrange("p (n t) -> p n t", t=P)[:, :, :rows], part,
                                  ALU.subtract).then_inc(lo_ready, 1)

            LINKS = 13

            def step(j, slots, rows):
                done = [0]

                def link(instruction):
                    done[0] += 1
                    instruction.then_inc(dve_step, 1)
                    dve.wait_ge(dve_step, START + j * 2 * LINKS + done[0])

                for s in slots:
                    negmax = og[s][:rows, :, HD].rearrange("p (g h) -> p g h", h=HEADS)
                    sums = og[s][:rows, :, HD + 1].rearrange("p (g h) -> p g h", h=HEADS)
                    dve.wait_ge(early_loaded[s], START + (j + 1) * 5 * 16)
                    link(dve.tensor_tensor(least[s][:rows, :], negmax[:, 0, :], negmax[:, 1, :], ALU.min))
                    link(dve.tensor_tensor(least[s][:rows, :], least[s][:rows, :], negmax[:, 2, :], ALU.min))
                    for g in range(GROUPS):
                        last = dve.tensor_tensor(share[s][:rows, g, :], least[s][:rows, :], negmax[:, g, :], ALU.subtract)
                    last.then_inc(share_asked[s], 1)
                for s in slots:
                    sums = og[s][:rows, :, HD + 1].rearrange("p (g h) -> p g h", h=HEADS)
                    dve.wait_ge(share_made[s], START + j + 1)
                    link(dve.tensor_tensor(shareL[s][:rows, :, :], share[s][:rows, :, :], sums, ALU.mult))
                    link(dve.tensor_tensor(total[s][:rows, :], shareL[s][:rows, 0, :], shareL[s][:rows, 1, :], ALU.add))
                    link(dve.tensor_tensor(total[s][:rows, :], total[s][:rows, :], shareL[s][:rows, 2, :], ALU.add))
                    link(dve.reciprocal(total[s][:rows, :], total[s][:rows, :]))
                    for g in range(GROUPS):
                        last = dve.tensor_tensor(share[s][:rows, g, :], share[s][:rows, g, :], total[s][:rows, :], ALU.mult)
                    link(last)
                    flat = share[s][:rows, :, :].rearrange("p g h -> p (g h)")
                    link(dve.tensor_tensor(og[s][:rows, :, :HD], og[s][:rows, :, :HD],
                                           flat.unsqueeze(2).to_broadcast([rows, GROUPS * HEADS, HD]), ALU.mult))
                    ob = og[s][:rows, 0:HEADS, :HD]
                    link(dve.tensor_tensor(ob, ob, og[s][:rows, HEADS:2 * HEADS, :HD], ALU.add))
                    link(dve.tensor_tensor(ob, ob, og[s][:rows, 2 * HEADS:3 * HEADS, :HD], ALU.add))
                    dve.wait_ge(silu_ready[s], START + (j + 1) * 2)
                    dve.tensor_tensor(dg[s][:rows, :, :], ob, dg[s][:rows, :, :], ALU.mult)
                    dve.wait_ge(rstd_a_ready[s], START + j + 1)
                    for h in range(HEADS):
                        last = dve.scalar_tensor_tensor(out=oa[s][:rows, h, :], in0=oa[s][:rows, h, :], scalar=rstd_a[s][:rows, h:h + 1],
                                                        in1=gg[s][:rows, h, :], op0=ALU.mult, op1=ALU.mult)
                    last.then_inc(z_ready[s], 1)
                for s in slots:
                    for n in range(3):
                        lo(j, slots, 0, s, n, zT[s][1][:, 4 * n:4 * n + 4, :rows], zT[s][0][:, 4 * n:4 * n + 4, :rows], rows)
                    lo(j, slots, 0, s, 3, peT[s][1][:, :, :rows], peT[s][0][:, :, :rows], rows)
                for s in slots:
                    dve.wait_ge(y_made[s], START + j + 1)
                    dve.wait_ge(gates_ready[s], START + (j + 1) * 2)
                    for n in range(2):
                        part = slice(n * BANK, (n + 1) * BANK)
                        dve.scalar_tensor_tensor(out=ga[s][:rows, part], in0=Y[n][:rows, :], scalar=1.0 / W_SCALE, in1=ga[s][:rows, part],
                                                 op0=ALU.mult, op1=ALU.mult)
                        last = dve.scalar_tensor_tensor(out=gb[s][:rows, part], in0=Y[2 + n][:rows, :], scalar=1.0 / W_SCALE,
                                                        in1=gb[s][:rows, part], op0=ALU.mult, op1=ALU.mult)
                    link(last)
                    dve.tensor_tensor(ga[s][:rows, :], ga[s][:rows, :], gb[s][:rows, :], ALU.add).then_inc(merged[s], 1)
                    for n in range(2):
                        lo(j, slots, 1, s, n, mT[s][1][:, 4 * n:4 * n + 4, :rows], mT[s][0][:, 4 * n:4 * n + 4, :rows], rows)
                for s in slots:
                    dve.wait_ge(rstd_m_ready[s], START + j + 1)
                    for n in range(2):
                        part = slice(n * BANK, (n + 1) * BANK)
                        last = dve.scalar_tensor_tensor(out=gb[s][:rows, part], in0=OUT[s][n][:rows, :], scalar=rstd_m[s][:rows, :],
                                                        in1=g_post_sb[:rows, part], op0=ALU.mult, op1=ALU.mult)
                    link(last)
                    dve.tensor_tensor(x[s][:rows, :], x[s][:rows, :], gb[s][:rows, :], ALU.add).then_inc(h_ready[s], 1)
                    for n in range(2):
                        lo(j, slots, 2, s, n, mT[s][1][:, 4 * n:4 * n + 4, :rows], mT[s][0][:, 4 * n:4 * n + 4, :rows], rows)
                for s in slots:
                    dve.wait_ge(proj_made[s], START + j + 1)
                    dve.wait_ge(gate_ready[s], START + (j + 1) * 2)
                    for n in range(2):
                        part = slice(n * BANK, (n + 1) * BANK)
                        last = dve.scalar_tensor_tensor(out=gb[s][:rows, part], in0=PROJ[s][n][:rows, :], scalar=1.0 / W_SCALE,
                                                        in1=gb[s][:rows, part], op0=ALU.mult, op1=ALU.mult)
                    link(last)
                    dve.tensor_tensor(x[s][:rows, :], x[s][:rows, :], gb[s][:rows, :], ALU.add).then_inc(y_ready[s], 1)
                assert done[0] == len(slots) * LINKS

            iterations(dve, step)

        @block.tensor
        def _(pe):
            pe.wait_ge(w_lo_ready, START + n_slices)

            def turn(j, slots, stage, s, n, blocks, rows):
                c, b = chunk(j, slots, stage, s, n)
                if isinstance(c, int) and c < 1:
                    pass
                elif stage == 0 and s == 0 and n == 0:
                    pe.wait_ge(lo_ready, START + j * PAIR_CHUNKS)
                else:
                    pe.wait_ge(lo_ready, START + c - 1)
                for i, src in enumerate(blocks):
                    last = pe.transpose(T[b][:, i * P:i * P + rows], src, identity[:rows, :rows])
                last.then_inc(turned, 1)

            def product(out, parts, name, slices, rows, signal=None):
                hi, lo = parts
                at = first[name]
                for k in range(slices):
                    for a, b in ((hi, w_hi), (hi, w_lo), (lo, w_hi)):
                        for n in range(2):
                            last = pe.matmul(out[n][:rows, :], a[:, k, :rows], b[:, at + k, n * BANK:(n + 1) * BANK],
                                             start=(k == 0 and a is hi and b is w_hi), stop=(k == slices - 1 and a is lo))
                if signal is not None:
                    last.then_inc(signal, 1)

            def step(j, slots, rows):
                for s in slots:
                    pe.wait_ge(z_ready[s], START + j + 1)
                    for n in range(2):
                        turn(j, slots, 0, s, n, [oa[s][:rows, 2 * n + i // 2, i % 2 * P:(i % 2 + 1) * P] for i in range(4)], rows)
                    turn(j, slots, 0, s, 2, [dg[s][:rows, i, :] for i in range(4)], rows)
                    turn(j, slots, 0, s, 3, [pe_in[s][:rows, i * P:(i + 1) * P] for i in range(2)], rows)
                    c, _ = chunk(j, slots, 0, s, 3)
                    pe.wait_ge(lo_ready, START + c + 1)
                    if s == 0:
                        pe.wait_ge(y_ready[0], START + j)
                        pe.wait_ge(y_ready[1], START + (j if slots == (0, 1) else PAIRS))
                    else:
                        pe.wait_ge(merged[0], START + j + 1)
                    product(Y[0:2], zT[s], "gla", GLA_VAL // P, rows)
                    product(Y[2:4], [part[:, GLA_VAL // P:, :] for part in zT[s]], "dil", WIDTH // P, rows, y_made[s])
                for s in slots:
                    pe.wait_ge(merged[s], START + j + 1)
                    for n in range(2):
                        turn(j, slots, 1, s, n, [ga[s][:rows, (4 * n + i) * P:(4 * n + i + 1) * P] for i in range(4)], rows)
                    c, _ = chunk(j, slots, 1, s, 1)
                    pe.wait_ge(lo_ready, START + c + 1)
                    product(OUT[s], mT[s], "out", K_TILES, rows, out_made[s])
                for s in slots:
                    pe.wait_ge(h_ready[s], START + j + 1)
                    for n in range(2):
                        turn(j, slots, 2, s, n, [x[s][:rows, (4 * n + i) * P:(4 * n + i + 1) * P] for i in range(4)], rows)
                    c, _ = chunk(j, slots, 2, s, 1)
                    pe.wait_ge(lo_ready, START + c + 1)
                    product(GATE[s], mT[s], "gate", K_TILES, rows, gate_made[s])
                    if s == 1:
                        pe.wait_ge(gate_ready[0], START + (j + 1) * 2)
                    product(PROJ[s], peT[s], "proj", PLE // P, rows, proj_made[s])

            iterations(pe, step)


def copy_new_rows(core, U, prompt_outs, sample_outs):
    nc = core.nc
    with ExitStack() as ctx:
        _, sem, _ = core.bind(ctx, "new_")
        copied = sem("copied")
        nc.all_engine_barrier()
        block = ctx.enter_context(nc.Block())

        @block.sync
        def _(sp):
            n = 0
            for g in range(GROUPS):
                for part, column in ((0, U_DK), (1, U_DV)):
                    window = prompt_outs[g].shape[2]
                    cols = slice(column + g * WIDTH, column + (g + 1) * WIDTH)
                    sp.dma_start(prompt_outs[g][0, 0, :, part].rearrange("l h d -> l (h d)"), U[SEQ - window:SEQ, cols]).then_inc(copied, 16)
                    sp.dma_start(sample_outs[g][0, :, window - DEC_SEQ:window, part].rearrange("b l h d -> b l (h d)"),
                                 U[SEQ:TOKENS, cols].rearrange("(b l) c -> b l c", b=DEC_BATCH)).then_inc(copied, 16)
                    n += 2
            sp.wait_ge(copied, START + 16 * n)


def build(nc, a, outs):
    y_prompt, y_sample, state_prompt, state_sample = outs[:4]
    kv_prompt, kv_sample = outs[4:7], outs[7:10]
    caches = [a["cache_kv_w128"], a["cache_kv_w512"], a["cache_kv_w2048"]]
    U = nc.dram_tensor("U", (TOKENS, U_WIDTH), F32).ap()
    OG = nc.dram_tensor("OG", (TOKENS, GROUPS, HEADS * (HD + 2)), F32).ap()
    OA = nc.dram_tensor("OA", (TOKENS, GLA_VAL), F32).ap()
    weights = [("gla", a["w_gla_branch"]), ("dil", a["w_dil_branch"]), ("out", a["w_out"]),
               ("gate", a["w_ple_gate"]), ("proj", a["w_ple_proj"])]
    core = Core(nc)
    with ExitStack() as whole:
        sb, _, _ = core.bind(whole)
        identity = sb("identity", [P, P])
        with ExitStack() as until_gla:
            sb, _, _ = core.bind(until_gla)
            lowrank = sb("lowrank", [LOWRANK + 1, TOKENS])
            decay_w = sb("decay_w", [LOWRANK + 1, GLA_KEY])
            with ExitStack() as until_projected:
                sb, sem, _ = core.bind(until_projected)
                xn_hi = sb("xn_hi", [P, K_TILES, TOKENS], F16)
                xn_lo = sb("xn_lo", [P, K_TILES, TOKENS], F16)
                raw = [sb(f"raw{s}", [P, K_TILES, BANK]) for s in range(2)]
                raw_loaded = [sem(f"raw_loaded{s}") for s in range(2)]
                w_view = a["w_in"][0].rearrange("(k p) n -> p k n", p=P)
                normalize_inputs(core, a["x_prompt"], a["x_sample"], a["g_pre"], w_view, raw, raw_loaded, identity, xn_hi, xn_lo)
                project_inputs(core, w_view, a["w_gla_lr"], a["b_gla_lr"], raw, raw_loaded, xn_hi, xn_lo, U, lowrank,
                               decay_w, list(zip(caches, kv_sample)))
            gla_recurrence(core, U, 0, GLA_CHUNK, SEQ // GLA_CHUNK, None, state_prompt[0], lowrank, decay_w,
                           a["causal_prompt"], a["starts_prompt"], identity, OA)
            gla_recurrence(core, U, SEQ, DEC_SEQ, DEC_BATCH, a["state_gla"][0], state_sample[0], lowrank, decay_w,
                           a["causal_sample"], a["starts_sample"], identity, OA)
        prompt_windows(core, U, a["window_mask"], identity, OG)
        sample_windows(core, U, caches, a["sample_mask"], identity, OG)
        copy_new_rows(core, U, kv_prompt, kv_sample)
        mix_outputs(core, U, OG, OA, a["x_prompt"], a["x_sample"], a["p_prompt"], a["p_sample"], weights,
                    a["g_gla_norm"], a["g_post"], identity, y_prompt, y_sample)


def constants():
    return {"window_mask": window_mask(), "sample_mask": sample_mask(),
            "causal_prompt": causal_mask(GLA_CHUNK), "causal_sample": causal_mask(DEC_SEQ),
            "starts_prompt": scan_starts(GLA_CHUNK), "starts_sample": scan_starts(DEC_SEQ)}


_INS = ["x_prompt", "x_sample", "state_gla", "cache_kv_w128", "cache_kv_w512", "cache_kv_w2048", "p_prompt", "p_sample",
        "g_pre", "g_post", "w_in", "w_gla_lr", "b_gla_lr", "g_gla_norm", "w_gla_branch", "w_dil_branch", "w_out",
        "w_ple_proj", "w_ple_gate"]
_OUTS = [(1, SEQ, D_MODEL), (DEC_BATCH, DEC_SEQ, D_MODEL), (1, 1, HEADS, GLA_DK, GLA_DV),
         (1, DEC_BATCH, HEADS, GLA_DK, GLA_DV)] \
    + [(1, 1, w, 2, HEADS, HD) for w, _ in WINDOWS] + [(1, DEC_BATCH, w, 2, HEADS, HD) for w, _ in WINDOWS]


def kernel(**inputs):
    import concourse.bacc as _bacc
    from concourse.bass_utils import run_bass_kernel_spmd as _run

    nc = _bacc.Bacc("TRN2", target_bir_lowering=False, num_devices=1)
    given = {name: np.ascontiguousarray(inputs[name]) for name in _INS} | constants()
    arrays, a = {}, {}
    for name, value in given.items():
        arrays[f"in_{name}"] = value
        a[name] = nc.dram_tensor(f"in_{name}", value.shape, mybir.dt.from_np(value.dtype), kind="ExternalInput").ap()
    outs = [nc.dram_tensor(f"out_{i}", shape, F32, kind="ExternalOutput").ap() for i, shape in enumerate(_OUTS)]
    build(nc, a, outs)
    r = _run(nc, [arrays], core_ids=[0])
    return tuple(r.results[0][f"out_{i}"] for i in range(len(_OUTS)))
```

```python
from contextlib import ExitStack

import numpy as np

import concourse.bass as bass
from concourse import mybir

F32 = mybir.dt.float32
F16 = mybir.dt.float16
ALU = mybir.AluOpType
ACT = mybir.ActivationFunctionType
AX_X = mybir.AxisListType.X

P = 128
BANK = 512
D_MODEL = 1024
SEQ = 2048
DEC_BATCH = 8
DEC_SEQ = 8
SAMPLES = DEC_BATCH * DEC_SEQ
TOKENS = SEQ + SAMPLES
TOKEN_TILES = -(-TOKENS // P)
K_TILES = D_MODEL // P
NORM_EPS = 1e-6

HEADS = 4
GLA_DK = 128
GLA_DV = 256
GLA_KEY = HEADS * GLA_DK
GLA_VAL = HEADS * GLA_DV
LOWRANK = 16
GLA_TAU = 16.0
GLA_CHUNK = 64

HD = 128
WIDTH = HEADS * HD
WINDOWS = ((128, 1), (512, 4), (2048, 16))
GROUPS = len(WINDOWS)
SPAN = 128
BLOCKS = SEQ // SPAN
SCALE = float(HD) ** -0.5
MASKED = -1e30

PLE = 256

W_LOWRANK = 2 * GLA_KEY + 2 * GLA_VAL
U_GQ = 0
U_GK = GLA_KEY
U_GV = 2 * GLA_KEY
U_GG = U_GV + GLA_VAL
U_DQ = U_GG + GLA_VAL
U_DK = U_DQ + GROUPS * WIDTH
U_DV = U_DK + GROUPS * WIDTH
U_DG = U_DV + GROUPS * WIDTH
U_GA = U_DG + WIDTH
U_GB = U_GA + D_MODEL
U_WIDTH = U_GB + D_MODEL
COLUMN_TILES = U_WIDTH // BANK
TILES_BEFORE_LOWRANK = W_LOWRANK // BANK

W_SCALE = 64.0

START = 1


def apart(eng):
    eng.nop(nofuse=True)


class Core:

    def __init__(self, nc):
        self.nc = nc

    def clear(self, sems):
        if sems:
            self.nc.clear_and_free_semaphores(sems)
            self.nc.all_engine_barrier()

    def bind(self, ctx, prefix=""):
        nc = self.nc
        sems = []
        ctx.callback(self.clear, sems)

        def sb(name, shape, dt=F32):
            return ctx.enter_context(nc.sbuf_tensor(prefix + name, shape, dt))

        def sem(name, start=START):
            sems.append(nc.alloc_semaphore(name=prefix + name))
            if start:
                nc.gpsimd.sem_inc(sems[-1], start)
            return sems[-1]

        def banks(name):
            return [ctx.enter_context(nc.psum_tensor(f"{prefix}{name}{b}", [P, BANK], F32)) for b in range(8)]

        return sb, sem, banks


def normalize_inputs(core, x_prompt, x_sample, g_pre, w_view, raw, raw_loaded, identity, xn_hi, xn_lo):
    nc = core.nc
    with ExitStack() as ctx:
        sb, sem, banks = core.bind(ctx)
        TILES = BANK // P
        x = [sb(f"x{s}", [P, TILES, D_MODEL]) for s in range(2)]
        squares = [sb(f"squares{s}", [P, D_MODEL]) for s in range(2)]
        g = sb("g", [P, K_TILES])
        mean = [sb(f"mean{s}", [P, TILES]) for s in range(2)]
        power = sb("power", [P, TILES])
        guarded = [sb(f"guarded{s}", [P, TILES]) for s in range(2)]
        rstd = [sb(f"rstd{s}", [P, TILES]) for s in range(2)]
        turned = banks("turned")
        g_loaded = sem("g_loaded")
        x_loaded = [[sem(f"x_loaded{s}{t}") for t in range(TILES)] for s in range(2)]
        squared = sem("squared")
        power_ready = sem("power_ready")
        guarded_ready = sem("guarded_ready")
        rstd_ready = sem("rstd_ready")
        scaled = sem("scaled")
        turned_ready = sem("turned_ready")
        hi_ready = sem("hi_ready")
        lo_ready = sem("lo_ready")
        ident_zero = sem("ident_zero")
        ident_ready = sem("ident_ready")
        GROUPS_X = [(TILES, P)] * (SEQ // BANK) + [(1, SAMPLES)]
        nc.all_engine_barrier()
        block = ctx.enter_context(nc.Block())

        def wait(eng, sem, n):
            if n > 0:
                eng.wait_ge(sem, START + n)

        @block.sync
        def _(sp):
            for i, (tiles, rows) in enumerate(GROUPS_X):
                wait(sp, turned_ready, (i - 1) * K_TILES)
                for t in range(tiles):
                    src = x_sample.rearrange("b t d -> (b t) d") if rows < P else x_prompt[0, i * BANK + t * P:i * BANK + (t + 1) * P, :]
                    sp.dma_start(x[i % 2][:rows, t, :], src).then_inc(x_loaded[i % 2][t], 16)
                if i == 0:
                    with nc.allow_non_contiguous_dma(reason="gains, once"):
                        sp.dma_start(g[:, :], g_pre[0].rearrange("(k p) -> p k", p=P)).then_inc(g_loaded, 16)
            for s in range(2):
                sp.dma_start(raw[s][:, :, :], w_view[:, :, s * BANK:(s + 1) * BANK]).then_inc(raw_loaded[s], 16)

        @block.gpsimd
        def _(pool):
            pool.memset(identity[:, :], 0.0).then_inc(ident_zero, 1)
            pool.wait_ge(ident_zero, START + 1)
            pool.affine_select(out=identity[:, :], in_=identity[:, :], compare_op=ALU.not_equal, fill=1.0,
                               base=0, pattern=[[-1, P]], channel_multiplier=1).then_inc(ident_ready, 1)
            pool.memset(power[:, :], -0.5).then_inc(power_ready, 1)
            pool.wait_ge(power_ready, START + 1)
            for i, (tiles, rows) in enumerate(GROUPS_X):
                s = i % 2
                pool.wait_ge(squared, START + i * TILES + tiles)
                pool.tensor_scalar(guarded[s][:rows, :tiles], mean[s][:rows, :tiles], NORM_EPS, None,
                                   ALU.add).then_inc(guarded_ready, 1)
                pool.wait_ge(guarded_ready, START + i + 1)
                wait(pool, scaled, (i - 1) * TILES)
                pool.tensor_tensor(rstd[s][:rows, :tiles], guarded[s][:rows, :tiles], power[:rows, :tiles],
                                   ALU.pow).then_inc(rstd_ready, 1)

        @block.scalar
        def _(act):
            def square(i):
                tiles, rows = GROUPS_X[i]
                wait(act, guarded_ready, i - 1)
                for t in range(tiles):
                    act.wait_ge(x_loaded[i % 2][t], START + (i // 2 + 1) * 16)
                    wait(act, squared, i * TILES + t - 1)
                    act.activation(squares[t % 2][:rows, :], x[i % 2][:rows, t, :], ACT.Square, scale=D_MODEL ** -0.5,
                                   accum_out=mean[i % 2][:rows, t:t + 1]).then_inc(squared, 1)

            square(0)
            act.wait_ge(g_loaded, START + 16)
            for i, (tiles, rows) in enumerate(GROUPS_X):
                if i + 1 < len(GROUPS_X):
                    square(i + 1)
                n = (tiles - 1) * P + rows
                for k in range(K_TILES):
                    act.wait_ge(turned_ready, START + i * K_TILES + k + 1)
                    act.activation(xn_hi[:, k, i * BANK:i * BANK + n], turned[k][:, :n], ACT.Copy,
                                   scale=g[:, k:k + 1]).then_inc(hi_ready, 1)

        @block.vector
        def _(dve):
            def scale(i):
                tiles, rows = GROUPS_X[i]
                dve.wait_ge(rstd_ready, START + i + 1)
                for t in range(tiles):
                    dve.tensor_scalar(x[i % 2][:rows, t, :], x[i % 2][:rows, t, :], rstd[i % 2][:rows, t:t + 1], None,
                                      ALU.mult).then_inc(scaled, 1)

            scale(0)
            dve.wait_ge(g_loaded, START + 16)
            for i, (tiles, rows) in enumerate(GROUPS_X):
                if i + 1 < len(GROUPS_X):
                    scale(i + 1)
                n = (tiles - 1) * P + rows
                for k in range(K_TILES):
                    dve.wait_ge(hi_ready, START + i * K_TILES + k + 1)
                    dve.scalar_tensor_tensor(out=xn_lo[:, k, i * BANK:i * BANK + n], in0=turned[k][:, :n],
                                             scalar=g[:, k:k + 1], in1=xn_hi[:, k, i * BANK:i * BANK + n],
                                             op0=ALU.mult, op1=ALU.subtract).then_inc(lo_ready, 1)

        @block.tensor
        def _(pe):
            pe.wait_ge(ident_ready, START + 1)
            for i, (tiles, rows) in enumerate(GROUPS_X):
                pe.wait_ge(scaled, START + i * TILES + tiles)
                for k in range(K_TILES):
                    wait(pe, lo_ready, (i - 1) * K_TILES + k + 1)
                    for t in range(tiles):
                        last = pe.transpose(turned[k][:, t * P:t * P + rows], x[i % 2][:rows, t, k * P:(k + 1) * P],
                                            identity[:rows, :rows])
                    last.then_inc(turned_ready, 1)


def project_inputs(core, w_view, raw, raw_loaded, xn_hi, xn_lo, U, L, shift_cache):
    nc = core.nc
    with ExitStack() as ctx:
        sb, sem, banks = core.bind(ctx)
        w_hi = [sb(f"w_hi{s}", [P, K_TILES, BANK], F16) for s in range(2)]
        w_lo = [sb(f"w_lo{s}", [P, K_TILES, BANK], F16) for s in range(2)]
        glr = sb("glr", [P, K_TILES, LOWRANK])
        lowrank = sb("lowrank", [LOWRANK + 1, TOKENS])
        glr_hi = sb("glr_hi", [P, K_TILES, LOWRANK], F16)
        glr_lo = sb("glr_lo", [P, K_TILES, LOWRANK], F16)
        stage = [[sb(f"stage{e}{s}", [P, BANK]) for s in range(2)] for e in range(2)]
        out = banks("out")
        glr_loaded = sem("glr_loaded")
        lowrank_stored = sem("lowrank_stored")
        ones_ready = sem("ones_ready")
        glr_cut = sem("glr_cut")
        glr_made = sem("glr_made")
        glr_kept = sem("glr_kept")
        hi_ready = [sem(f"w_hi_ready{s}") for s in range(2)]
        lo_ready = [sem(f"w_lo_ready{s}") for s in range(2)]
        out_ready = [sem(f"out_ready{e}") for e in range(2)]
        staged = [sem(f"staged{e}") for e in range(2)]
        stored = [[sem(f"stored{e}{s}") for s in range(2)] for e in range(2)]
        copied = sem("copied", start=0)
        ITERS = COLUMN_TILES // 2
        LOWRANK_CHUNKS = -(-TOKENS // BANK)
        M = 2 * TOKEN_TILES
        PER = M // 2
        ROWS = [P] * (TOKEN_TILES - 1) + [TOKENS - (TOKEN_TILES - 1) * P]
        USES = [(PER + 1) // 2, PER // 2]
        nc.all_engine_barrier()
        block = ctx.enter_context(nc.Block())

        def shift(eng, cache, out, b):
            window = cache.shape[2]
            return eng.dma_start(out[0, bass.ds(b, 1), 0:window - DEC_SEQ].rearrange("b l k h d -> b l (k h d)"),
                                 cache[0, bass.ds(b, 1), DEC_SEQ:window].rearrange("b l k h d -> b l (k h d)"))

        @block.sync
        def _(sp):
            with nc.allow_non_contiguous_dma(reason="low-rank columns, once"):
                sp.dma_start(glr[:, :, :], w_view[:, :, W_LOWRANK:W_LOWRANK + LOWRANK]).then_inc(glr_loaded, 16)

            def step(i, skip, last=False):
                for s in range(2):
                    if not last:
                        sp.wait_ge(lo_ready[s], START + i + 1)
                        sp.dma_start(raw[s][:, :, :], w_view[:, :, bass.ds((i + 1) * 2 * BANK + s * BANK + skip, BANK)]) \
                            .then_inc(raw_loaded[s], 16)
                    for t in range(TOKEN_TILES):
                        m = s * TOKEN_TILES + t
                        e, j = m % 2, m // 2
                        sp.wait_ge(staged[e], START + i * PER + j + 1)
                        sp.dma_start(U[t * P:t * P + ROWS[t], bass.ds(i * 2 * BANK + s * BANK, BANK)],
                                     stage[e][j % 2][:ROWS[t], :]).then_inc(stored[e][j % 2], 16)

            before = TILES_BEFORE_LOWRANK // 2 - 1
            with sp.Fori(0, before) as i:
                step(i, 0)
            with sp.Fori(before, ITERS - 1) as i:
                step(i, LOWRANK)
            step(ITERS - 1, LOWRANK, last=True)
            sp.wait_ge(glr_kept, START + LOWRANK_CHUNKS)
            sp.dma_start(L[:, :], lowrank[:, :]).then_inc(lowrank_stored, 16)
            for e in range(2):
                for s in range(2):
                    sp.wait_ge(stored[e][s], START + ITERS * USES[s] * 16)
            sp.wait_ge(lowrank_stored, START + 16)

        @block.gpsimd
        def _(pool):
            pool.memset(lowrank[:, :], 1.0).then_inc(ones_ready, 1)
            with pool.Fori(0, DEC_BATCH) as i:
                pool.wait_ge(raw_loaded[1], START + (i + 2) * 16)
                for cache, out in shift_cache:
                    shift(pool, cache, out, i).then_inc(copied, 16)
            pool.wait_ge(copied, DEC_BATCH * len(shift_cache) * 16)

        first = 0

        def was_last(i, s):
            return i * PER - PER + (TOKEN_TILES - 1) // 2 + 1 if s == 0 else i * PER

        def evacuate(eng, e, i, m, write):
            s, t = divmod(m, TOKEN_TILES)
            j = m // 2
            eng.wait_ge(out_ready[e], START + i * PER + j + 1)
            eng.wait_ge(stored[e][j % 2], START + (i * USES[j % 2] + j // 2) * 16)
            write(stage[e][j % 2][:ROWS[t], :], out[m % 8][:ROWS[t], :]).then_inc(staged[e], 1)

        @block.scalar
        def _(act):
            act.wait_ge(glr_loaded, START + 16)
            act.activation(glr_hi[:, :, :], glr[:, :, :], ACT.Copy, scale=W_SCALE).then_inc(glr_cut, 1)

            def cut(i, s):
                act.wait_ge(raw_loaded[s], START + (i + 1) * 16)
                if s == 1 or i is not first:
                    act.wait_ge(out_ready[s], START + was_last(i, s))
                act.activation(w_hi[s][:, :, :], raw[s][:, :, :], ACT.Copy, scale=W_SCALE).then_inc(hi_ready[s], 1)

            def step(i, last=False):
                for m in range(M):
                    if m == 0:
                        cut(i, 1)
                    if m == TOKEN_TILES and not last:
                        cut(i + 1, 0)
                    if m % 2 == 0:
                        evacuate(act, 0, i, m, lambda o, x: act.activation(o, x, ACT.Copy, scale=1.0 / W_SCALE))

            cut(first, 0)
            with act.Fori(0, ITERS - 1) as i:
                step(i)
            step(ITERS - 1, last=True)

        @block.vector
        def _(dve):
            dve.wait_ge(glr_loaded, START + 16)
            dve.wait_ge(glr_cut, START + 1)
            dve.scalar_tensor_tensor(out=glr_lo[:, :, :], in0=glr[:, :, :], scalar=W_SCALE, in1=glr_hi[:, :, :],
                                     op0=ALU.mult, op1=ALU.subtract).then_inc(glr_cut, 1)
            dve.wait_ge(ones_ready, START + 1)
            for c in range(LOWRANK_CHUNKS):
                n = min(BANK, TOKENS - c * BANK)
                dve.wait_ge(glr_made, START + c + 1)
                dve.tensor_scalar(lowrank[0:LOWRANK, c * BANK:c * BANK + n], out[c][0:LOWRANK, :n], 1.0 / W_SCALE, None,
                                  ALU.mult).then_inc(glr_kept, 1)

            def cut(i, s):
                dve.wait_ge(hi_ready[s], START + i + 1)
                if s == 1 or i is not first:
                    dve.wait_ge(out_ready[s], START + was_last(i, s))
                dve.scalar_tensor_tensor(out=w_lo[s][:, :, :], in0=raw[s][:, :, :], scalar=W_SCALE, in1=w_hi[s][:, :, :],
                                         op0=ALU.mult, op1=ALU.subtract).then_inc(lo_ready[s], 1)

            def step(i, last=False):
                for m in range(M):
                    if m == 0:
                        cut(i, 1)
                    if m == TOKEN_TILES and not last:
                        cut(i + 1, 0)
                    if m % 2 == 1:
                        evacuate(dve, 1, i, m, lambda o, x: dve.tensor_scalar(o, x, 1.0 / W_SCALE, None, ALU.mult))

            cut(first, 0)
            with dve.Fori(0, ITERS - 1) as i:
                step(i)
            step(ITERS - 1, last=True)

        @block.tensor
        def _(pe):
            pe.wait_ge(glr_cut, START + 2)
            for c in range(LOWRANK_CHUNKS):
                n = min(BANK, TOKENS - c * BANK)
                for k in range(K_TILES):
                    for a, b in ((glr_hi, xn_hi), (glr_hi, xn_lo), (glr_lo, xn_hi)):
                        last = pe.matmul(out[c][0:LOWRANK, :n], a[:, k, :], b[:, k, c * BANK:c * BANK + n],
                                         start=(k == 0 and a is glr_hi and b is xn_hi), stop=(k == K_TILES - 1 and a is glr_lo))
                last.then_inc(glr_made, 1)
            pe.wait_ge(glr_kept, START + LOWRANK_CHUNKS)
            with pe.Fori(0, ITERS) as i:
                for s in range(2):
                    pe.wait_ge(hi_ready[s], START + i + 1)
                    pe.wait_ge(lo_ready[s], START + i + 1)
                    for t in range(TOKEN_TILES):
                        m = s * TOKEN_TILES + t
                        pe.wait_ge(staged[m % 2], START + (i * PER + (m - 8) // 2 + 1 if m >= 8 else i * PER))
                        rows, at = ROWS[t], t * P
                        for k in range(K_TILES):
                            passes = ((xn_hi, w_hi[s]), (xn_hi, w_lo[s]), (xn_lo, w_hi[s]))
                            for n, (a, b) in enumerate(passes):
                                last = pe.matmul(out[m % 8][:rows, :], a[:, k, at:at + rows], b[:, k, :],
                                                 start=(k == 0 and n == 0), stop=(k == K_TILES - 1 and n == 2))
                        last.then_inc(out_ready[m % 2], 1)


def prompt_windows(core, U, window_mask, identity, OG, prompt_outs, sample_outs):
    nc = core.nc
    with ExitStack() as ctx:
        sb, sem, banks = core.bind(ctx)
        q = [sb(f"q{g}", [P, BLOCKS, HD]) for g in range(GROUPS)]
        k = [sb(f"k{g}", [P, BLOCKS, HD]) for g in range(GROUPS)]
        v = [sb(f"v{g}", [P, BLOCKS, HD]) for g in range(GROUPS)]
        qkT = [sb(f"qkT{g}", [P, BLOCKS, 2, P]) for g in range(GROUPS)]
        result = [sb(f"result{g}", [P, BLOCKS, HD + 2]) for g in range(GROUPS)]
        mask = sb("mask", [P, 2, P])
        score = [sb(f"score{s}", [P, 2, P]) for s in range(2)]
        prob = [sb(f"prob{s}", [P, 2, P]) for s in range(2)]
        probT = [sb(f"probT{s}", [P, 2, P]) for s in range(2)]
        top = [sb(f"top{s}", [P, 1]) for s in range(2)]
        bank = banks("win")
        mask_loaded = sem("mask_loaded")
        loaded = [sem(f"qkv_loaded{g}") for g in range(GROUPS)]
        stored = [sem(f"result_stored{g}") for g in range(GROUPS)]
        turned = sem("qk_turned")
        turned_kept = sem("qk_kept")
        scored = sem("scored")
        masked = sem("masked")
        top_ready = sem("top_ready")
        weighed = sem("weighed")
        prob_turned = sem("prob_turned")
        prob_kept = sem("prob_kept")
        summed = sem("summed")
        result_kept = sem("result_kept")
        rows_copied = sem("rows_copied", start=0)
        STEPS = GROUPS * BLOCKS
        nc.all_engine_barrier()
        block = ctx.enter_context(nc.Block())

        def tokens(dram, g):
            dil = WINDOWS[g][1]
            return dram.rearrange("(n i r) c -> i n r c", i=SPAN, r=dil)

        def rings(tile, g):
            dil = WINDOWS[g][1]
            return tile.rearrange("p (n r) c -> p n r c", r=dil)

        def done(h, s, lag=0):
            return h * STEPS + max(s - lag + 1, 0)

        def first_key_block(s):
            g, b = divmod(s, BLOCKS)
            return 0 if b >= WINDOWS[g][1] else 1

        @block.sync
        def _(sp):
            sp.dma_start(mask[:, :, :], window_mask.rearrange("p (a j) -> p a j", a=2)).then_inc(mask_loaded, 16)

            def load(h, g):
                for tile, column in ((q[g], U_DQ), (k[g], U_DK), (v[g], U_DV)):
                    src = tokens(U[0:SEQ, bass.ds(h * HD + column + g * WIDTH, HD)], g)
                    dst = rings(tile[:, :, :], g)
                    for n in range(BLOCKS // WINDOWS[g][1]):
                        sp.dma_start(dst[:, n], src[:, n]).then_inc(loaded[g], 16)

            def step(h, last=False):
                for g in range(GROUPS):
                    sp.wait_ge(result_kept, START + done(h, (g + 1) * BLOCKS - 1))
                    dst = tokens(OG[0:SEQ, g, bass.ds(h * (HD + 2), HD + 2)], g)
                    src = rings(result[g][:, :, :], g)
                    for n in range(BLOCKS // WINDOWS[g][1]):
                        sp.dma_start(dst[:, n], src[:, n]).then_inc(stored[g], 16)
                    if not last:
                        load(h + 1, g)

            for g in range(GROUPS):
                load(0, g)
            with sp.Fori(0, HEADS - 1) as h:
                step(h)
            step(HEADS - 1, last=True)
            for g in range(GROUPS):
                sp.wait_ge(stored[g], START + HEADS * 16 * (BLOCKS // WINDOWS[g][1]))

        @block.gpsimd
        def _(pool):
            for g in range(GROUPS):
                pool.wait_ge(loaded[g], START + 3 * 16 * (BLOCKS // WINDOWS[g][1]))
            for g in range(GROUPS):
                for part, column in ((0, U_DK), (1, U_DV)):
                    window = prompt_outs[g].shape[2]
                    cols = slice(column + g * WIDTH, column + (g + 1) * WIDTH)
                    pool.dma_start(prompt_outs[g][0, 0, :, part].rearrange("l h d -> l (h d)"),
                                   U[SEQ - window:SEQ, cols]).then_inc(rows_copied, 16)
                    pool.dma_start(sample_outs[g][0, :, window - DEC_SEQ:window, part].rearrange("b l h d -> b l (h d)"),
                                   U[SEQ:TOKENS, cols].rearrange("(b l) c -> b l c", b=DEC_BATCH)).then_inc(rows_copied, 16)
            pool.wait_ge(rows_copied, 2 * 2 * GROUPS * 16)

        @block.tensor
        def _(pe):
            def turn(h, s):
                g, b = divmod(s, BLOCKS)
                if b == 0:
                    pe.wait_ge(loaded[g], START + (h + 1) * 3 * 16 * (BLOCKS // WINDOWS[g][1]))
                pe.wait_ge(turned_kept, START + done(h, s, 2))
                pe.transpose(bank[s % 2][:, 0:P], q[g][:, b, :], identity[:, :])
                pe.transpose(bank[s % 2][:, P:2 * P], k[g][:, b, :], identity[:, :]).then_inc(turned, 1)

            def scores(h, s):
                g, b = divmod(s, BLOCKS)
                dil, a = WINDOWS[g][1], first_key_block(s)
                pe.wait_ge(turned_kept, START + done(h, s))
                pe.wait_ge(masked, START + done(h, s, 2))
                keys = qkT[g][:, b - dil:b + 1:dil, 1, :] if a == 0 else qkT[g][:, b:b + 1, 1, :]
                out = bank[2 + s % 2][:, a * P:2 * P].rearrange("p (a j) -> p a j", j=P)
                pe.matmul(out, qkT[g][:, b, 0, :], keys, start=True, stop=True).then_inc(scored, 1)

            def turn_prob(h, s):
                pe.wait_ge(weighed, START + done(h, s))
                pe.wait_ge(prob_kept, START + done(h, s, 2))
                for a in range(first_key_block(s), 2):
                    last = pe.transpose(bank[4 + s % 2][:, a * P:(a + 1) * P], prob[s % 2][:, a, :], identity[:, :])
                last.then_inc(prob_turned, 1)

            def values(h, s):
                g, b = divmod(s, BLOCKS)
                dil, first = WINDOWS[g][1], first_key_block(s)
                pe.wait_ge(prob_kept, START + done(h, s))
                pe.wait_ge(result_kept, START + done(h, s, 2))
                for a in range(first, 2):
                    last = pe.matmul(bank[6 + s % 2][:, :HD], probT[s % 2][:, a, :], v[g][:, b - dil * (1 - a), :],
                                     start=(a == first), stop=(a == 1))
                last.then_inc(summed, 1)

            with pe.Fori(0, HEADS) as h:
                for s in range(STEPS + 4):
                    if s < STEPS:
                        turn(h, s)
                    if 1 <= s < STEPS + 1:
                        scores(h, s - 1)
                    if 3 <= s < STEPS + 3:
                        turn_prob(h, s - 3)
                    if s >= 4:
                        values(h, s - 4)

        @block.scalar
        def _(act):
            def keep_turned(h, s):
                g, b = divmod(s, BLOCKS)
                act.wait_ge(turned, START + done(h, s))
                act.wait_ge(scored, START + h * STEPS)
                act.activation(qkT[g][:, b, :, :], bank[s % 2][:, :2 * P].rearrange("p (a j) -> p a j", j=P),
                               ACT.Copy).then_inc(turned_kept, 1)

            def weigh(h, s):
                g, b = divmod(s, BLOCKS)
                a = first_key_block(s)
                if b == 0:
                    act.wait_ge(stored[g], START + h * 16 * (BLOCKS // WINDOWS[g][1]))
                act.wait_ge(top_ready, START + done(h, s))
                act.wait_ge(prob_turned, START + done(h, s, 2))
                act.activation(prob[s % 2][:, a:, :], score[s % 2][:, a:, :], ACT.Exp, scale=SCALE,
                               bias=result[g][:, b, HD:HD + 1], accum_out=result[g][:, b, HD + 1:HD + 2]).then_inc(weighed, 1)

            with act.Fori(0, HEADS) as h:
                for s in range(STEPS + 2):
                    if s < STEPS:
                        keep_turned(h, s)
                    if s >= 2:
                        weigh(h, s - 2)

        @block.vector
        def _(dve):
            dve.wait_ge(mask_loaded, START + 16)

            def mask_scores(h, s):
                g, b = divmod(s, BLOCKS)
                a = first_key_block(s)
                if b == 0:
                    dve.wait_ge(stored[g], START + h * 16 * (BLOCKS // WINDOWS[g][1]))
                dve.wait_ge(scored, START + done(h, s))
                dve.wait_ge(weighed, START + done(h, s, 2))
                apart(dve)
                dve.tensor_tensor_reduce(score[s % 2][:, a:, :],
                                         bank[2 + s % 2][:, a * P:2 * P].rearrange("p (a j) -> p a j", j=P),
                                         mask[:, a:, :], 1.0, MASKED, ALU.add, ALU.max, top[s % 2][:, :]).then_inc(masked, 1)
                dve.wait_ge(masked, START + done(h, s))
                dve.tensor_scalar(result[g][:, b, HD:HD + 1], top[s % 2][:, :], -SCALE, None,
                                  ALU.mult).then_inc(top_ready, 1)

            def keep_prob(h, s):
                dve.wait_ge(prob_turned, START + done(h, s))
                dve.wait_ge(summed, START + done(h, s, 2))
                a = first_key_block(s)
                dve.tensor_copy(probT[s % 2][:, a:, :],
                                bank[4 + s % 2][:, a * P:2 * P].rearrange("p (a j) -> p a j", j=P)).then_inc(prob_kept, 1)

            def keep_result(h, s):
                g, b = divmod(s, BLOCKS)
                dve.wait_ge(summed, START + done(h, s))
                dve.tensor_copy(result[g][:, b, :HD], bank[6 + s % 2][:, :HD]).then_inc(result_kept, 1)

            with dve.Fori(0, HEADS) as h:
                for s in range(STEPS + 4):
                    if 1 <= s < STEPS + 1:
                        mask_scores(h, s - 1)
                    if 3 <= s < STEPS + 3:
                        keep_prob(h, s - 3)
                    if s >= 4:
                        keep_result(h, s - 4)


def window_mask():
    i, j = np.arange(SPAN)[:, None], np.arange(SPAN)[None, :]
    before = np.where(j >= i, 0.0, MASKED)
    own = np.where(j <= i, 0.0, MASKED)
    return np.concatenate([before, own], axis=1).astype(np.float32)


def gla_recurrence(core, U, row0, C, halves, steps, state_in, state_out, L, w_lr, b_lr, causal, starts, identity, OA,
                   cutter=None):
    nc = core.nc
    carried = state_in is None
    with ExitStack() as ctx:
        sb, sem, banks = core.bind(ctx, "prompt_" if carried else "sample_")
        T = halves * C
        wide = [P, HEADS, halves, C]
        qk = [sb(f"qk{s}", [T, 2 * GLA_KEY]) for s in range(2)]
        v = [sb(f"v{s}", [T, GLA_VAL]) for s in range(2)]
        z = sb("z", wide)
        log_a = sb("log_a", wide)
        decay = sb("decay", wide)
        grow = sb("grow", wide)
        to_end = sb("to_end", wide)
        shrink, end_decay = decay, to_end
        q_in = [sb(f"q_in{s}", wide) for s in range(2)]
        k_inv = sb("k_inv", wide)
        k_end = sb("k_end", wide)
        q_late = sb("q_late", [P, HEADS, C])
        k_early = sb("k_early", [P, HEADS, C])
        carry = [sb(f"carry{s}", [P, HEADS]) for s in range(2)]
        att = [sb(f"att{s}", [T, HEADS, T]) for s in range(2)]
        k_endT = [sb(f"k_endT{s}", [T, HEADS, P]) for s in range(2)]
        o = [sb(f"o{s}", [T, GLA_VAL]) for s in range(2)]
        state = [sb(f"state{s}", [P, HEADS, GLA_DV]) for s in range(2)]
        new_state = [state[1], state[0]] if carried else [sb(f"new_state{s}", [P, HEADS, GLA_DV]) for s in range(2)]
        lowrank = sb("lowrank", [LOWRANK + 1, steps * T])
        decay_w = sb("decay_w", [LOWRANK + 1, GLA_KEY])
        causal_sb = sb("causal_sb", [T, HEADS, T])
        starts_sb = sb("starts_sb", [P, HEADS * T])
        bank = banks("gla")
        Q, K, Z, ATT, O, S = bank[0], bank[1], bank[2], bank[3], bank[4:6], bank[6:8]
        KE = S[0]
        const_loaded = sem("const_loaded")
        decay_loaded = sem("decay_loaded")
        zeroed = sem("zeroed")
        qk_loaded = [sem(f"qk_loaded{s}") for s in range(2)]
        v_loaded = [sem(f"v_loaded{s}") for s in range(2)]
        state_loaded = [sem(f"state_loaded{s}") for s in range(2)]
        o_stored = [sem(f"o_stored{s}") for s in range(2)]
        state_stored = [sem(f"state_stored{s}") for s in range(2)]
        z_made = sem("z_made")
        qk_turned = sem("qk_turned")
        z_abs_ready = sem("z_abs_ready")
        z_exp_ready = sem("z_exp_ready")
        z_log_ready = sem("z_log_ready")
        log_a_ready = sem("log_a_ready")
        decay_ready = sem("decay_ready")
        to_end_ready = sem("to_end_ready")
        grow_ready = sem("grow_ready")
        end_ready = sem("end_ready")
        shrink_ready = sem("shrink_ready")
        crossing_ready = sem("crossing_ready")
        scaled = sem("scaled")
        att_made = sem("att_made")
        k_end_turned = sem("k_end_turned")
        att_kept = sem("att_kept")
        k_end_kept = sem("k_end_kept")
        products = sem("state_products")
        state_ready = sem("state_ready")
        o_made = sem("o_made")
        o_kept = sem("o_kept")
        nc.all_engine_barrier()
        block = ctx.enter_context(nc.Block())

        def wait(eng, sem, n):
            if not isinstance(n, int) or n > 0:
                eng.wait_ge(sem, START + n)

        def pipeline(eng, decays, prepare, attend, finish):
            def ahead(j, s):
                if eng is nc.vector:
                    finish(j, s)
                    decays(j + 1, s)
                else:
                    decays(j + 1, s)
                    finish(j, s)

            decays(0, 0)
            prepare(0, 0)
            decays(0, 1)
            with eng.Fori(0, steps // 2 - 1) as j:
                attend(j, 0)
                prepare(j, 1)
                ahead(j, 0)
                attend(j, 1)
                prepare(j + 1, 0)
                ahead(j, 1)
            j = steps // 2 - 1
            attend(j, 0)
            prepare(j, 1)
            finish(j, 0)
            attend(j, 1)
            finish(j, 1)

        def rows(j, s):
            return bass.ds(j * (2 * T) + (row0 + s * T), T)

        def flat(tile):
            return tile[:, :, :, :].rearrange("p h b c -> p (h b c)") if len(tile.shape) == 4 else tile[:, :, :].rearrange("p h c -> p (h c)")

        def part(bank, half):
            return bank[:, :HEADS * T].rearrange("p (h b c) -> p h b c", h=HEADS, b=halves)[:, :, half, :]

        @block.sync
        def _(sp):
            sp.dma_start(lowrank[:, :], L[:, row0:row0 + steps * T]).then_inc(decay_loaded, 16)
            sp.dma_start(decay_w[0:LOWRANK, :], w_lr[0]).then_inc(decay_loaded, 16)
            sp.dma_start(decay_w[LOWRANK:LOWRANK + 1, :], b_lr).then_inc(decay_loaded, 16)

            def load(j, s):
                c = 2 * j + s
                wait(sp, qk_turned, c - 1)
                sp.dma_start(qk[s][:, :], U[rows(j, s), U_GQ:U_GQ + 2 * GLA_KEY]).then_inc(qk_loaded[s], 16)
                if isinstance(j, int) and c == 0:
                    sp.dma_start(starts_sb[:, :], starts).then_inc(const_loaded, 16)
                    sp.dma_start(causal_sb[:, :, :], causal.rearrange("p (h c) -> p h c", c=T)).then_inc(const_loaded, 16)
                wait(sp, o_made, c - 1)
                sp.dma_start(v[s][:, :], U[rows(j, s), U_GV:U_GV + GLA_VAL]).then_inc(v_loaded[s], 16)
                if not carried:
                    wait(sp, state_ready, c - 1)
                    sp.dma_start(state[s][:, :, :], state_in[bass.ds(c, 1)].rearrange("b h d e -> d (b h) e")).then_inc(state_loaded[s], 16)

            def store(j, s):
                c = 2 * j + s
                sp.wait_ge(o_kept, START + c + 1)
                sp.dma_start(OA[rows(j, s), :], o[s][:, :]).then_inc(o_stored[s], 16)
                if not carried:
                    sp.wait_ge(state_ready, START + c + 1)
                    sp.dma_start(state_out[bass.ds(c, 1)].rearrange("b h d e -> d (b h) e"), new_state[s][:, :, :]).then_inc(state_stored[s], 16)

            load(0, 0)
            load(0, 1)
            if cutter is not None:
                cutter.load(sp, 0, 0)
            last = steps // 2 - 1
            with sp.Fori(0, last) as j:
                for s in range(2):
                    if cutter is not None:
                        cutter.load(sp, j + s, 1 - s)
                    load(j + 1, s)
                    store(j, s)
            if cutter is not None:
                cutter.load(sp, last, 1)
            store(last, 0)
            store(last, 1)
            if carried:
                sp.wait_ge(state_ready, START + steps)
                sp.dma_start(state_out[0].rearrange("h d e -> d h e"), state[steps % 2][:, :, :]).then_inc(state_stored[0], 16)
                sp.wait_ge(state_stored[0], START + 16)
            for s in range(2):
                sp.wait_ge(o_stored[s], START + steps // 2 * 16)
                if not carried:
                    sp.wait_ge(state_stored[s], START + steps // 2 * 16)

        if cutter is not None:
            @block.gpsimd
            def _(pool):
                cutter.program(pool)

        @block.tensor
        def _(pe):
            if carried:
                pe.wait_ge(zeroed, START + 3)
            pe.wait_ge(decay_loaded, START + 48)

            def decays(j, s):
                c = 2 * j + s
                wait(pe, log_a_ready, c)
                for h in range(HEADS):
                    last = pe.matmul(Z[:, h * T:(h + 1) * T], decay_w[:, h * P:(h + 1) * P], lowrank[:, bass.ds(j * (2 * T) + s * T, T)],
                                     start=True, stop=True)
                last.then_inc(z_made, 1)

            def prepare(j, s):
                c = 2 * j + s
                pe.wait_ge(qk_loaded[s], START + 16 * j + 16)
                wait(pe, scaled, c)
                apart(pe)
                for n in range(2 * HEADS):
                    h = n % HEADS
                    last = pe.transpose((Q if n < HEADS else K)[:, h * T:(h + 1) * T], qk[s][:, n * P:(n + 1) * P], identity[:T, :T])
                last.then_inc(qk_turned, 1)

            def attend(j, s):
                c = 2 * j + s
                pe.wait_ge(scaled, START + c + 1)
                wait(pe, att_kept, c)
                wait(pe, state_ready, c)
                apart(pe)
                for h in range(HEADS):
                    last = pe.transpose(KE[:T, h * P:(h + 1) * P], k_end[:, h, :, :].rearrange("p b c -> p (b c)"), identity[:, :])
                last.then_inc(k_end_turned, 1)
                for h in range(HEADS):
                    last = pe.matmul(ATT[:C, h * T:h * T + C], k_inv[:, h, 0, :], q_in[s][:, h, 0, :], start=True, stop=True)
                    if halves == 2:
                        pe.matmul(ATT[:C, h * T + C:(h + 1) * T], k_early[:, h, :], q_late[:, h, :], start=True, stop=True)
                        last = pe.matmul(ATT[C:T, h * T + C:(h + 1) * T], k_inv[:, h, 1, :], q_late[:, h, :], start=True, stop=True)
                last.then_inc(att_made, 1)

            def finish(j, s):
                c = 2 * j + s
                pe.wait_ge(v_loaded[s], START + 16 * j + 16)
                pe.wait_ge(k_end_kept, START + c + 1)
                apart(pe)
                for h in range(HEADS):
                    last = pe.matmul(S[h // 2][:, h % 2 * GLA_DV:(h % 2 + 1) * GLA_DV], k_endT[s][:, h, :],
                                     v[s][:, h * GLA_DV:(h + 1) * GLA_DV], start=True, stop=True)
                last.then_inc(products, 1)
                pe.wait_ge(att_kept, START + c + 1)
                wait(pe, o_kept, c)
                if not carried:
                    pe.wait_ge(state_loaded[s], START + 16 * j + 16)
                apart(pe)
                for h in range(HEADS):
                    out = O[h // 2][:T, h % 2 * GLA_DV:(h % 2 + 1) * GLA_DV]
                    pe.matmul(out, att[s][:, h, :], v[s][:, h * GLA_DV:(h + 1) * GLA_DV], start=True, stop=False)
                    last = pe.matmul(out, q_in[s][:, h, :, :].rearrange("p b c -> p (b c)"), state[s][:, h, :], start=False, stop=True)
                last.then_inc(o_made, 1)

            pipeline(pe, decays, prepare, attend, finish)

        @block.scalar
        def _(act):
            def decays(j, s):
                c = 2 * j + s
                act.wait_ge(z_made, START + c + 1)
                wait(act, log_a_ready, c)
                act.activation(flat(z), Z[:, :HEADS * T], ACT.Abs).then_inc(z_abs_ready, 1)
                act.wait_ge(z_abs_ready, START + c + 1)
                act.activation(flat(z), flat(z), ACT.Exp, scale=-1.0).then_inc(z_exp_ready, 1)
                act.wait_ge(z_exp_ready, START + c + 1)
                act.activation(flat(z), flat(z), ACT.Ln, bias=1.0).then_inc(z_log_ready, 1)

            def prepare(j, s):
                c = 2 * j + s
                act.wait_ge(decay_ready, START + c + 1)
                wait(act, scaled, c)
                act.activation(flat(grow), flat(decay), ACT.Exp, scale=1.0 / GLA_TAU).then_inc(grow_ready, 1)
                act.wait_ge(to_end_ready, START + c + 1)
                act.activation(flat(end_decay), flat(to_end), ACT.Exp, scale=1.0 / GLA_TAU).then_inc(end_ready, 1)
                act.wait_ge(grow_ready, START + c + 1)
                act.activation(flat(shrink), flat(decay), ACT.Exp, scale=-1.0 / GLA_TAU).then_inc(shrink_ready, 1)

            def attend(j, s):
                c = 2 * j + s
                act.wait_ge(k_end_turned, START + c + 1)
                wait(act, products, 2 * j)
                act.activation(flat(k_endT[s]), KE[:T, :], ACT.Copy).then_inc(k_end_kept, 1)
                if cutter is not None:
                    cutter.high(act, j, s)

            def finish(j, s):
                c = 2 * j + s
                act.wait_ge(o_made, START + c + 1)
                wait(act, o_stored[s], 16 * j)
                act.activation(o[s][:, 0:BANK], O[0][:T, :], ACT.Copy)
                act.activation(o[s][:, BANK:2 * BANK], O[1][:T, :], ACT.Copy).then_inc(o_kept, 1)

            pipeline(act, decays, prepare, attend, finish)

        @block.vector
        def _(dve):
            for s in range(2):
                dve.memset(att[s][:, :, :], 0.0).then_inc(zeroed, 1)
            if carried:
                dve.memset(state[0][:, :, :], 0.0).then_inc(zeroed, 1)
            dve.wait_ge(zeroed, START + (3 if carried else 2))
            dve.wait_ge(const_loaded, START + 32)

            def decays(j, s):
                c = 2 * j + s
                dve.wait_ge(z_log_ready, START + c + 1)
                dve.scalar_tensor_tensor(out=flat(log_a), in0=Z[:, :HEADS * T], scalar=0.0, in1=flat(z),
                                         op0=ALU.min, op1=ALU.subtract).then_inc(log_a_ready, 1)

            def prepare(j, s):
                c = 2 * j + s
                dve.wait_ge(log_a_ready, START + c + 1)
                dve.tensor_tensor_scan(flat(decay), starts_sb[:, :], flat(log_a), 0.0,
                                       ALU.mult, ALU.add).then_inc(decay_ready, 1)
                dve.wait_ge(decay_ready, START + c + 1)
                dve.tensor_tensor(to_end[:, :, :, :], decay[:, :, :, C - 1:C].to_broadcast(wide), decay[:, :, :, :],
                                  ALU.subtract).then_inc(to_end_ready, 1)
                if cutter is not None and not (isinstance(j, int) and c == 0):
                    cutter.low(dve, j + s - 1, 1 - s)
                dve.wait_ge(qk_turned, START + c + 1)
                dve.wait_ge(grow_ready, START + c + 1)
                wait(dve, o_made, c - 1)
                scale = GLA_DK ** -0.5
                if halves == 2:
                    dve.scalar_tensor_tensor(out=q_late[:, :, :], in0=part(Q, 1), scalar=scale, in1=grow[:, :, 1, :],
                                             op0=ALU.mult, op1=ALU.mult).then_inc(crossing_ready, 1)
                dve.scalar_tensor_tensor(out=q_in[s][:, :, 0, :], in0=part(Q, 0), scalar=scale, in1=grow[:, :, 0, :],
                                         op0=ALU.mult, op1=ALU.mult)
                dve.wait_ge(end_ready, START + c + 1)
                dve.tensor_tensor(k_end[:, :, halves - 1, :], part(K, halves - 1), end_decay[:, :, halves - 1, :], ALU.mult)
                ends = [grow[:, :, b, C - 1:C] for b in range(halves)]
                if halves == 2:
                    dve.tensor_tensor(k_early[:, :, :], part(K, 0), end_decay[:, :, 0, :], ALU.mult).then_inc(crossing_ready, 1)
                    dve.wait_ge(crossing_ready, START + c * 2 + 2)
                    dve.tensor_tensor(q_in[s][:, :, 1, :], q_late[:, :, :], ends[0].to_broadcast([P, HEADS, C]), ALU.mult)
                    dve.tensor_tensor(k_end[:, :, 0, :], k_early[:, :, :], ends[1].to_broadcast([P, HEADS, C]), ALU.mult)
                    dve.tensor_tensor(carry[s][:, :].unsqueeze(2), ends[0], ends[1], ALU.mult)
                else:
                    dve.tensor_copy(carry[s][:, :].unsqueeze(2), ends[0])
                dve.wait_ge(shrink_ready, START + c + 1)
                dve.tensor_tensor(flat(k_inv), K[:, :HEADS * T], flat(shrink), ALU.mult).then_inc(scaled, 1)

            def attend(j, s):
                c = 2 * j + s
                dve.wait_ge(att_made, START + c + 1)
                wait(dve, o_made, 2 * j)
                apart(dve)
                last = dve.copy_predicated(flat(att[s])[:C], flat(causal_sb)[:C].bitcast(mybir.dt.int32), ATT[:C, :HEADS * T])
                if halves == 2:
                    late = ATT[C:T, :HEADS * T].rearrange("p (h t) -> p h t", h=HEADS)[:, :, C:T]
                    last = dve.copy_predicated(att[s][C:T, :, C:T], causal_sb[C:T, :, C:T].bitcast(mybir.dt.int32), late)
                last.then_inc(att_kept, 1)

            def finish(j, s):
                c = 2 * j + s
                dve.wait_ge(products, START + c + 1)
                if carried:
                    wait(dve, o_made, c)
                else:
                    dve.wait_ge(state_loaded[s], START + 16 * j + 16)
                    wait(dve, state_stored[s], 16 * j)
                for h in range(HEADS):
                    last = dve.scalar_tensor_tensor(out=new_state[s][:, h, :], in0=state[s][:, h, :],
                                                    scalar=carry[s][:, h:h + 1],
                                                    in1=S[h // 2][:, h % 2 * GLA_DV:(h % 2 + 1) * GLA_DV],
                                                    op0=ALU.mult, op1=ALU.add)
                last.then_inc(state_ready, 1)

            pipeline(dve, decays, prepare, attend, finish)
            if cutter is not None:
                cutter.low(dve, steps // 2 - 1, 1)


def causal_mask(T):
    one = (np.arange(T)[:, None] <= np.arange(T)[None, :]).astype(np.float32)
    return np.tile(one, (1, HEADS))


def scan_starts(C, halves):
    row = np.ones((HEADS * halves, C), np.float32)
    row[:, 0] = 0.0
    return np.broadcast_to(row.reshape(1, -1), (P, HEADS * halves * C)).copy()


CACHE_BLOCKS = [(g, r) for g, (_, dil) in enumerate(WINDOWS) for r in range(min(dil, DEC_SEQ))]
N_CACHE = len(CACHE_BLOCKS)
N_BLOCKS = N_CACHE + 1
NEW_KEYS = GROUPS * DEC_SEQ
KEYS = N_CACHE * P + NEW_KEYS
QUAD = 32
PER_BANK = BANK // P
SCORE_BANKS = -(-N_BLOCKS // PER_BANK)


def sample_mask():
    mask = np.full((P, KEYS), MASKED, np.float32)
    for t in range(DEC_SEQ):
        one = np.full(KEYS, MASKED, np.float32)
        for n, (g, r) in enumerate(CACHE_BLOCKS):
            window, dil = WINDOWS[g]
            back = window + t - (np.arange(P) * dil + r)
            one[n * P:(n + 1) * P][(back % dil == 0) & (back <= window)] = 0.0
        for g, (window, dil) in enumerate(WINDOWS):
            back = t - np.arange(DEC_SEQ)
            one[N_CACHE * P + g * DEC_SEQ:][:DEC_SEQ][(back >= 0) & (back % dil == 0)] = 0.0
        mask[t::QUAD] = one
    return mask


def sample_windows(core, U, caches, mask_in, identity, OG):
    nc = core.nc
    with ExitStack() as ctx:
        sb, sem, banks = core.bind(ctx, "sw_")
        kv = [[sb(f"kv{s}_{n}", [P, 2 * WIDTH]) for n in range(N_CACHE)] for s in range(2)]
        kv_new = [sb(f"kv_new{s}", [NEW_KEYS, 2 * WIDTH]) for s in range(2)]
        q = [sb(f"q{s}", [DEC_SEQ, GROUPS * WIDTH]) for s in range(2)]
        qT = [sb(f"qT{s}", [P, GROUPS * HEADS, QUAD]) for s in range(2)]
        kT = [sb(f"kT{s}", [P, HEADS, P]) for s in range(2)]
        prob = [sb(f"prob{s}", [P, KEYS]) for s in range(2)]
        probT = [sb(f"probT{s}", [P, N_BLOCKS, P]) for s in range(2)]
        mask = sb("mask", [P, KEYS])
        tops = [sb(f"tops{s}", [P, SCORE_BANKS]) for s in range(2)]
        top = [sb(f"top{s}", [P, 1]) for s in range(2)]
        result = [sb(f"result{s}", [P, HD + 2]) for s in range(2)]
        empty = sb("empty", [SAMPLES, (GROUPS - 1) * HEADS, HD + 2])
        bank = banks("sw")
        KT, SC, PT, Q, O = bank[0:2], bank[2:4], bank[4:6], bank[6], bank[7]
        mask_loaded = sem("mask_loaded")
        zeroed = sem("zeroed")
        empty_stored = sem("empty_stored")
        q_loaded = [sem(f"q_loaded{s}") for s in range(2)]
        kv_loaded = [[sem(f"kv_loaded{s}_{n}") for n in range(N_BLOCKS)] for s in range(2)]
        q_turned = sem("q_turned")
        q_kept = sem("q_kept")
        k_turned = sem("k_turned")
        k_kept = sem("k_kept")
        block_scored = sem("block_scored")
        masked = sem("masked")
        topped = sem("topped")
        top_ready = sem("top_ready")
        weighed = sem("weighed")
        p_turned = sem("p_turned")
        p_kept = sem("p_kept")
        summed = sem("summed")
        o_kept = sem("o_kept")
        o_stored = [sem(f"o_stored{s}") for s in range(2)]
        PAIRS = DEC_BATCH // 2
        nc.all_engine_barrier()
        block = ctx.enter_context(nc.Block())

        def widths(m):
            blocks = range(m * PER_BANK, min((m + 1) * PER_BANK, N_BLOCKS))
            return blocks, min(BANK, KEYS - m * BANK)

        @block.sync
        def _(sp):
            sp.dma_start(mask[:, :], mask_in).then_inc(mask_loaded, 16)
            sp.wait_ge(zeroed, START + 4)
            with nc.allow_non_contiguous_dma(reason="once"):
                sp.dma_start(OG[SEQ:TOKENS, 1:GROUPS, :], empty[:, :, :].rearrange("t (g h) c -> t g (h c)", h=HEADS)) \
                    .then_inc(empty_stored, 16)

            def load(j, s):
                c = 2 * j + s
                rows = bass.ds(c * DEC_SEQ + SEQ, DEC_SEQ)
                sp.dma_start(q[s][:, :], U[rows, U_DQ:U_DQ + GROUPS * WIDTH]).then_inc(q_loaded[s], 16)
                for n, (g, r) in enumerate(CACHE_BLOCKS):
                    window, dil = WINDOWS[g]
                    src = caches[g][0, bass.ds(c, 1)].rearrange("b (l r) k h d -> r l (b k h d)", r=dil)
                    sp.dma_start(kv[s][n][:, :], src[r]).then_inc(kv_loaded[s][n], 16)
                for g in range(GROUPS):
                    for part, column in ((0, U_DK), (1, U_DV)):
                        sp.dma_start(kv_new[s][g * DEC_SEQ:(g + 1) * DEC_SEQ, part * WIDTH:(part + 1) * WIDTH],
                                     U[rows, column + g * WIDTH:column + (g + 1) * WIDTH]).then_inc(kv_loaded[s][N_CACHE], 16)

            def store(j, s):
                c = 2 * j + s
                sp.wait_ge(o_kept, START + c + 1)
                for h in range(HEADS):
                    rows = bass.ds(c * DEC_SEQ + SEQ, DEC_SEQ)
                    sp.dma_start(OG[rows, 0, h * (HD + 2):(h + 1) * (HD + 2)], result[s][h * QUAD:h * QUAD + DEC_SEQ, :]).then_inc(o_stored[s], 16)

            def step(j, last=False):
                for s in range(2):
                    sp.wait_ge(summed, START + 2 * j + s + 1)
                    if not last:
                        load(j + 1, s)
                for s in range(2):
                    store(j, s)

            load(0, 0)
            load(0, 1)
            with sp.Fori(0, PAIRS - 1) as j:
                step(j)
            step(PAIRS - 1, last=True)
            for s in range(2):
                sp.wait_ge(o_stored[s], START + PAIRS * HEADS * 16)
            sp.wait_ge(empty_stored, START + 16)

        @block.gpsimd
        def _(pool):
            for s in range(2):
                pool.memset(qT[s][:, :, :], 0.0).then_inc(zeroed, 1)
            pool.memset(empty[:, :, :], 0.0).then_inc(zeroed, 1)
            pool.wait_ge(zeroed, START + 3)
            pool.memset(empty[:, :, HD:HD + 1], -MASKED).then_inc(zeroed, 1)

        @block.tensor
        def _(pe):
            pe.wait_ge(zeroed, START + 4)

            def query(j, s):
                c = 2 * j + s
                pe.wait_ge(q_loaded[s], START + 16 * j + 16)
                pe.wait_ge(q_kept, START + c)
                apart(pe)
                for n in range(GROUPS * HEADS):
                    last = pe.transpose(Q[:, n * DEC_SEQ:(n + 1) * DEC_SEQ], q[s][:, n * P:(n + 1) * P], identity[:DEC_SEQ, :DEC_SEQ])
                last.then_inc(q_turned, 1)

            def turn_keys(j, s, n):
                c = 2 * j + s
                pe.wait_ge(kv_loaded[s][n], START + ((16 * j + 16) * (1 if n < N_CACHE else 2 * GROUPS)))
                pe.wait_ge(k_kept, START + c * N_BLOCKS + max(n - 1, 0))
                keys, src = (P, kv[s][n]) if n < N_CACHE else (NEW_KEYS, kv_new[s])
                apart(pe)
                for h in range(HEADS):
                    last = pe.transpose(KT[n % 2][:, h * P:h * P + keys], src[:, h * P:(h + 1) * P], identity[:keys, :keys])
                last.then_inc(k_turned, 1)

            def score(j, s, n):
                c = 2 * j + s
                m = n // PER_BANK
                pe.wait_ge(k_kept, START + c * N_BLOCKS + n + 1)
                if n == 0:
                    pe.wait_ge(q_kept, START + c + 1)
                if n % PER_BANK == 0:
                    pe.wait_ge(masked, START + c * SCORE_BANKS + max(m - 1, 0))
                for h in range(HEADS):
                    at = n % PER_BANK * P
                    out = SC[m % 2][h * QUAD:(h + 1) * QUAD, :]
                    if n < N_CACHE:
                        g = CACHE_BLOCKS[n][0]
                        last = pe.matmul(out[:, at:at + P], qT[s][:, g * HEADS + h, :], kT[n % 2][:, h, :], start=True, stop=True)
                    else:
                        for g in range(GROUPS):
                            last = pe.matmul(out[:, at + g * DEC_SEQ:at + (g + 1) * DEC_SEQ], qT[s][:, g * HEADS + h, :],
                                             kT[n % 2][:, h, g * DEC_SEQ:(g + 1) * DEC_SEQ], start=True, stop=True)
                last.then_inc(block_scored, 1)

            def turn_prob(j, s, m):
                c = 2 * j + s
                pe.wait_ge(weighed, START + c + 1)
                pe.wait_ge(p_kept, START + c * SCORE_BANKS + max(m - 1, 0))
                blocks, _ = widths(m)
                for n in blocks:
                    keys = P if n < N_CACHE else NEW_KEYS
                    last = pe.transpose(PT[m % 2][:keys, n % PER_BANK * P:(n % PER_BANK + 1) * P],
                                        prob[s][:, n * P:n * P + keys], identity[:, :])
                last.then_inc(p_turned, 1)

            def values(j, s):
                c = 2 * j + s
                pe.wait_ge(p_kept, START + (c + 1) * SCORE_BANKS)
                pe.wait_ge(o_kept, START + c)
                for n in range(N_BLOCKS):
                    keys, src = (P, kv[s][n]) if n < N_CACHE else (NEW_KEYS, kv_new[s])
                    for h in range(HEADS):
                        last = pe.matmul(O[h * QUAD:(h + 1) * QUAD, :HD], probT[s][:keys, n, h * QUAD:(h + 1) * QUAD],
                                         src[:, WIDTH + h * HD:WIDTH + (h + 1) * HD], start=(n == 0), stop=(n == N_BLOCKS - 1))
                last.then_inc(summed, 1)

            with pe.Fori(0, PAIRS) as j:
                for s in range(2):
                    query(j, s)
                    for n in range(N_BLOCKS + 1):
                        if n < N_BLOCKS:
                            turn_keys(j, s, n)
                        if n:
                            score(j, s, n - 1)
                for s in range(2):
                    for m in range(SCORE_BANKS):
                        turn_prob(j, s, m)
                    values(j, s)

        @block.scalar
        def _(act):
            def keep_keys(j, s, n):
                c = 2 * j + s
                act.wait_ge(k_turned, START + c * N_BLOCKS + n + 1)
                act.wait_ge(block_scored, START + c * N_BLOCKS + max(n - 1, 0))
                keys = P if n < N_CACHE else NEW_KEYS
                act.activation(kT[n % 2][:, :, :keys], KT[n % 2][:, :].rearrange("p (h k) -> p h k", h=HEADS)[:, :, :keys],
                               ACT.Copy).then_inc(k_kept, 1)

            def weigh(j, s):
                c = 2 * j + s
                act.wait_ge(top_ready, START + c + 1)
                act.activation(prob[s][:, :], prob[s][:, :], ACT.Exp, scale=SCALE, bias=result[s][:, HD:HD + 1],
                               accum_out=result[s][:, HD + 1:HD + 2]).then_inc(weighed, 1)

            with act.Fori(0, PAIRS) as j:
                for s in range(2):
                    for n in range(N_BLOCKS):
                        keep_keys(j, s, n)
                    weigh(j, s)

        @block.vector
        def _(dve):
            dve.wait_ge(mask_loaded, START + 16)
            dve.wait_ge(zeroed, START + 4)

            def keep_query(j, s):
                c = 2 * j + s
                dve.wait_ge(q_turned, START + c + 1)
                dve.tensor_copy(qT[s][:, :, :DEC_SEQ], Q[:, :GROUPS * HEADS * DEC_SEQ].rearrange("p (n t) -> p n t", t=DEC_SEQ)) \
                   .then_inc(q_kept, 1)

            def mask_scores(j, s, m):
                c = 2 * j + s
                blocks, w = widths(m)
                dve.wait_ge(block_scored, START + c * N_BLOCKS + blocks[-1] + 1)
                if m == 0:
                    dve.wait_ge(o_stored[s], START + j * HEADS * 16)
                    dve.wait_ge(p_turned, START + 2 * j * SCORE_BANKS)
                apart(dve)
                dve.tensor_tensor_reduce(prob[s][:, m * BANK:m * BANK + w], SC[m % 2][:, :w], mask[:, m * BANK:m * BANK + w],
                                         1.0, MASKED, ALU.add, ALU.max, tops[s][:, m:m + 1]).then_inc(masked, 1)

            def find_top(j, s):
                c = 2 * j + s
                dve.wait_ge(masked, START + (c + 1) * SCORE_BANKS)
                dve.tensor_reduce(top[s][:, :], tops[s][:, :], AX_X, ALU.max).then_inc(topped, 1)
                dve.wait_ge(topped, START + c + 1)
                dve.tensor_scalar(result[s][:, HD:HD + 1], top[s][:, :], -SCALE, None, ALU.mult).then_inc(top_ready, 1)

            def keep_prob(j, s, m):
                c = 2 * j + s
                dve.wait_ge(p_turned, START + c * SCORE_BANKS + m + 1)
                dve.wait_ge(summed, START + 2 * j)
                blocks, _ = widths(m)
                full = [n for n in blocks if n < N_CACHE]
                src = PT[m % 2][:, :].rearrange("p (n k) -> p n k", k=P)
                last = dve.tensor_copy(probT[s][:, full[0]:full[-1] + 1, :], src[:, :len(full), :])
                if len(full) < len(blocks):
                    last = dve.tensor_copy(probT[s][:NEW_KEYS, N_CACHE, :], src[:NEW_KEYS, len(full), :])
                last.then_inc(p_kept, 1)

            def keep_output(j, s):
                c = 2 * j + s
                dve.wait_ge(summed, START + c + 1)
                dve.tensor_copy(result[s][:, :HD], O[:, :HD]).then_inc(o_kept, 1)

            with dve.Fori(0, PAIRS) as j:
                for s in range(2):
                    keep_query(j, s)
                    for m in range(SCORE_BANKS):
                        mask_scores(j, s, m)
                    find_top(j, s)
                for s in range(2):
                    for m in range(SCORE_BANKS):
                        keep_prob(j, s, m)
                    keep_output(j, s)


class Cutter:

    def __init__(self, core, whole, weights, g_gla, shared):
        self.core, self.g_gla = core, g_gla
        self.views, self.first, self.slices, n = {}, {}, {}, 0
        for name, w in weights:
            self.views[name] = w[0].rearrange("(k p) n -> p k n", p=P)
            self.first[name], self.slices[name] = n, w.shape[1] // P
            n += self.slices[name]
        self.shared = shared
        self.alone = [name for name, _ in weights if name not in shared]
        sb, _, _ = core.bind(whole, "cut_")
        self.hi = sb("w_hi", [P, n, D_MODEL], F16)
        self.lo = sb("w_lo", [P, n, D_MODEL], F16)

    def begin(self, ctx):
        sb, sem, _ = self.core.bind(ctx, "cut_")
        self.raw = sb("raw", [P, D_MODEL])
        self.own_raw = [sb(f"own_raw{d}", [P, D_MODEL]) for d in range(2)]
        self.gains = sb("gains", [P, GLA_VAL // P])
        self.gains_ready = sem("gains_ready")
        self.gains_loaded = sem("gains_loaded", start=0)
        self.own_loaded = [sem(f"own_loaded{d}", start=0) for d in range(2)]
        self.own_scaled = sem("own_scaled")
        self.own_hi = sem("own_hi")
        self.own_lo = [sem(f"own_lo{d}") for d in range(2)]
        self.loaded = [sem(f"loaded{s}") for s in range(2)]
        self.hi_cut = [sem(f"hi_cut{s}") for s in range(2)]
        self.lo_cut = [sem(f"lo_cut{s}") for s in range(2)]
        return self

    def piece(self, part, name, k):
        return part[:, bass.ds(k + self.first[name], 1), :].rearrange("p k n -> p (k n)")

    def load(self, sp, j, s):
        if s == 1 or not isinstance(j, int) or j > 0:
            sp.wait_ge(self.lo_cut[1 - s], START + (j + s))
        view = self.views[self.shared[s]][:, bass.ds(j, 1), :].rearrange("p k n -> p (k n)")
        sp.dma_start(self.raw[:, :], view).then_inc(self.loaded[s], 16)

    def high(self, act, j, s):
        act.wait_ge(self.loaded[s], START + 16 * j + 16)
        act.activation(self.piece(self.hi, self.shared[s], j), self.raw[:, :], ACT.Copy,
                       scale=W_SCALE).then_inc(self.hi_cut[s], 1)

    def low(self, dve, j, s):
        dve.wait_ge(self.hi_cut[s], START + j + 1)
        dve.scalar_tensor_tensor(out=self.piece(self.lo, self.shared[s], j), in0=self.raw[:, :], scalar=W_SCALE,
                                 in1=self.piece(self.hi, self.shared[s], j), op0=ALU.mult, op1=ALU.subtract).then_inc(self.lo_cut[s], 1)

    def program(self, pool):
        with self.core.nc.allow_non_contiguous_dma(reason="gains, once"):
            pool.dma_start(self.gains[:, :], self.g_gla[0].rearrange("(k p) -> p k", p=P)).then_inc(self.gains_loaded, 16)
        pool.wait_ge(self.gains_loaded, 16)
        pool.tensor_scalar(self.gains[:, :], self.gains[:, :], W_SCALE, None, ALU.mult).then_inc(self.gains_ready, 1)
        pool.wait_ge(self.gains_ready, START + 1)

        def cut(name, k, done):
            for d in range(2):
                if not isinstance(done, int) or done > 0:
                    pool.wait_ge(self.own_lo[d], START + done)
                view = self.views[name][:, bass.ds(k * 2 + d, 1), :].rearrange("p k n -> p (k n)")
                pool.dma_start(self.own_raw[d][:, :], view).then_inc(self.own_loaded[d], 16)
            for d in range(2):
                raw, hi, lo = self.own_raw[d], self.piece(self.hi, name, k * 2 + d), self.piece(self.lo, name, k * 2 + d)
                scale = self.gains[:, k * 2 + d:k * 2 + d + 1] if name == "gla" else W_SCALE
                pool.wait_ge(self.own_loaded[d], done * 16 + 16)
                apart(pool)
                pool.tensor_scalar(raw[:, :], raw[:, :], scale, None, ALU.mult).then_inc(self.own_scaled, 1)
                pool.wait_ge(self.own_scaled, START + done * 2 + d + 1)
                pool.tensor_copy(hi, raw[:, :]).then_inc(self.own_hi, 1)
                pool.wait_ge(self.own_hi, START + done * 2 + d + 1)
                pool.tensor_tensor(lo, raw[:, :], hi, ALU.subtract).then_inc(self.own_lo[d], 1)

        before = 0
        for name in self.alone:
            pairs = self.slices[name] // 2
            if name == "gla":
                for k in range(pairs):
                    cut(name, k, before + k)
            else:
                with pool.Fori(0, pairs) as k:
                    cut(name, k, k + before)
            before += pairs
        for d in range(2):
            pool.wait_ge(self.own_lo[d], START + before)


def mix_outputs(core, U, OG, OA, x_prompt, x_sample, p_prompt, p_sample, w_hi, w_lo, first, g_post, identity, y_prompt, y_sample):
    nc = core.nc
    with ExitStack() as ctx:
        sb, sem, banks = core.bind(ctx, "mix_")
        N_Z = (GLA_VAL + WIDTH) // P
        og = [sb(f"og{s}", [P, GROUPS * HEADS, HD + 2]) for s in range(2)]
        oa = [sb(f"oa{s}", [P, HEADS, GLA_DV]) for s in range(2)]
        gg = [sb(f"gg{s}", [P, HEADS, GLA_DV]) for s in range(2)]
        dg = [sb(f"dg{s}", [P, HEADS, HD]) for s in range(2)]
        ga = [sb(f"ga{s}", [P, D_MODEL]) for s in range(2)]
        gb = [sb(f"gb{s}", [P, D_MODEL]) for s in range(2)]
        x = [sb(f"x{s}", [P, D_MODEL]) for s in range(2)]
        pe_in = [sb(f"pe{s}", [P, PLE]) for s in range(2)]
        zT = [[sb(f"zT{s}{part}", [P, N_Z, P], F16) for part in "hl"] for s in range(2)]
        mT = [[sb(f"mT{s}{part}", [P, K_TILES, P], F16) for part in "hl"] for s in range(2)]
        peT = [[sb(f"peT{s}{part}", [P, PLE // P, P], F16) for part in "hl"] for s in range(2)]
        g_post_sb = sb("g_post_sb", [P, D_MODEL])
        junk = sb("junk", [P, BANK], F16)
        power = sb("power", [P, HEADS])
        least = [sb(f"least{s}", [P, HEADS]) for s in range(2)]
        share = [sb(f"share{s}", [P, GROUPS, HEADS]) for s in range(2)]
        shareL = [sb(f"shareL{s}", [P, GROUPS, HEADS]) for s in range(2)]
        total = [sb(f"total{s}", [P, HEADS]) for s in range(2)]
        mean_a = [sb(f"mean_a{s}", [P, HEADS]) for s in range(2)]
        rstd_a = [sb(f"rstd_a{s}", [P, HEADS]) for s in range(2)]
        mean_m = [sb(f"mean_m{s}", [P, 2]) for s in range(2)]
        rstd_m = [sb(f"rstd_m{s}", [P, 1]) for s in range(2)]
        bank = banks("mix")
        T, B0, B1, B2 = bank[0:2], bank[2:4], bank[4:6], bank[6:8]
        YA, YB, OUT, PROJ, GATE = [B0, B2], [B1, B0], [B1, B2], [B0, B2], [B1, B1]

        def per_slot(name):
            return [sem(f"{name}{s}") for s in range(2)]

        g_loaded = sem("g_loaded")
        power_ready = sem("power_ready")
        early_loaded = per_slot("early_loaded")
        late_loaded = per_slot("late_loaded")
        y_stored = per_slot("y_stored")
        prepare_step = per_slot("prepare_step")
        products_gated = per_slot("products_gated")
        out_scaled = per_slot("out_scaled")
        ple_gated = per_slot("ple_gated")
        guarded_a = per_slot("guarded_a")
        m_step = per_slot("m_step")
        share_asked = per_slot("share_asked")
        share_made = per_slot("share_made")
        mean_a_ready = per_slot("mean_a_ready")
        rstd_a_ready = per_slot("rstd_a_ready")
        silu_ready = per_slot("silu_ready")
        gates_ready = per_slot("gates_ready")
        z_ready = per_slot("z_ready")
        y_made = per_slot("y_made")
        merged = per_slot("merged")
        out_made = per_slot("out_made")
        mean_m_ready = per_slot("mean_m_ready")
        rstd_m_ready = per_slot("rstd_m_ready")
        h_ready = per_slot("h_ready")
        gate_made = per_slot("gate_made")
        gate_ready = per_slot("gate_ready")
        proj_made = per_slot("proj_made")
        y_ready = per_slot("y_ready")
        turned = sem("turned")
        hi_ready = sem("hi_ready")
        lo_ready = sem("lo_ready")
        PAIRS = SEQ // P // 2
        nc.all_engine_barrier()
        block = ctx.enter_context(nc.Block())

        Z_CHUNKS, PER = 4, 16
        FULL = {("m", 0): 0, ("m", 1): 2, ("h", 0): 4, ("z", 0): 6, ("h", 1): 10, ("z", 1): 12}
        ALONE = {("m", 0): 0, ("h", 0): 2}

        def chunk(j, stage, s, n):
            if isinstance(j, int) and j == -1:
                return s * Z_CHUNKS + n
            if isinstance(j, int) and j == PAIRS:
                return 2 * Z_CHUNKS + PAIRS * PER - Z_CHUNKS + ALONE[stage, s] + n
            return j * PER + (2 * Z_CHUNKS + FULL[stage, s] + n)

        def iterations(eng, before, step):
            before()
            with eng.Fori(0, PAIRS - 1) as j:
                step(j, (0, 1), P, (0, 1), P)
            step(PAIRS - 1, (0, 1), P, (0,), SAMPLES)
            step(PAIRS, (0,), SAMPLES, (), 0)

        def tile_rows(tile):
            return bass.ds(tile * P, P)

        @block.sync
        def _(sp):
            sp.dma_start(g_post_sb[:, :], g_post.to_broadcast([P, D_MODEL])).then_inc(g_loaded, 16)

            def early(pair, s, rows):
                at = tile_rows(pair * 2 + s) if rows == P else slice(SEQ, TOKENS)
                sp.dma_start(og[s][:rows, :, :], OG[at].rearrange("t g (h c) -> t (g h) c", h=HEADS)).then_inc(early_loaded[s], 16)
                sp.dma_start(oa[s][:rows, :, :], OA[at].rearrange("t (h c) -> t h c", h=HEADS)).then_inc(early_loaded[s], 16)
                sp.dma_start(gg[s][:rows, :, :], U[at, U_GG:U_GG + GLA_VAL].rearrange("t (h c) -> t h c", h=HEADS)).then_inc(early_loaded[s], 16)
                sp.dma_start(dg[s][:rows, :, :], U[at, U_DG:U_DG + WIDTH].rearrange("t (h c) -> t h c", h=HEADS)).then_inc(early_loaded[s], 16)
                src = p_prompt[0, 0, at, :] if rows == P else p_sample[0].rearrange("b t d -> (b t) d")
                sp.dma_start(pe_in[s][:rows, :], src).then_inc(early_loaded[s], 16)

            def late(pair, s, rows):
                at = tile_rows(pair * 2 + s) if rows == P else slice(SEQ, TOKENS)
                sp.dma_start(ga[s][:rows, :], U[at, U_GA:U_GA + D_MODEL]).then_inc(late_loaded[s], 16)
                sp.dma_start(gb[s][:rows, :], U[at, U_GB:U_GB + D_MODEL]).then_inc(late_loaded[s], 16)
                src = x_prompt[0, at, :] if rows == P else x_sample.rearrange("b t d -> (b t) d")
                sp.dma_start(x[s][:rows, :], src).then_inc(late_loaded[s], 16)

            def step(j, slots, early_rows, late_rows):
                for s in slots:
                    if s in early_rows:
                        sp.wait_ge(turned, START + chunk(j, "z", s, Z_CHUNKS - 1) + 1)
                        early(j + 2, s, early_rows[s])
                    sp.wait_ge(y_ready[s], START + j + 1)
                    if isinstance(j, int) and j == PAIRS:
                        sp.dma_start(y_sample.rearrange("b t d -> (b t) d"), x[s][:SAMPLES, :]).then_inc(y_stored[s], 16)
                    else:
                        sp.dma_start(y_prompt[0, tile_rows(2 * j + s), :], x[s][:, :]).then_inc(y_stored[s], 16)
                    if s in late_rows:
                        sp.wait_ge(y_stored[s], START + (j + 1) * 16)
                        late(j + 1, s, late_rows[s])

            for s in range(2):
                early(0, s, P)
            for s in range(2):
                late(0, s, P)
            for s in range(2):
                sp.wait_ge(turned, START + chunk(-1, "z", s, Z_CHUNKS - 1) + 1)
                early(1, s, P)
            with sp.Fori(0, PAIRS - 2) as j:
                step(j, (0, 1), {0: P, 1: P}, {0: P, 1: P})
            step(PAIRS - 2, (0, 1), {0: SAMPLES}, {0: P, 1: P})
            step(PAIRS - 1, (0, 1), {}, {0: SAMPLES})
            step(PAIRS, (0,), {}, {})
            sp.wait_ge(y_stored[0], START + (PAIRS + 1) * 16)
            sp.wait_ge(y_stored[1], START + PAIRS * 16)

        @block.gpsimd
        def _(pool):
            pool.memset(power[:, :], -0.5).then_inc(power_ready, 1)
            pool.wait_ge(power_ready, START + 1)

            def norm_a(q, s, rows):
                pool.wait_ge(mean_a_ready[s], START + (q + 1) * HEADS)
                apart(pool)
                pool.tensor_scalar(mean_a[s][:rows, :], mean_a[s][:rows, :], NORM_EPS, None, ALU.add).then_inc(guarded_a[s], 1)
                pool.wait_ge(guarded_a[s], START + q + 1)
                pool.wait_ge(z_ready[s], START + q)
                pool.tensor_tensor(rstd_a[s][:rows, :], mean_a[s][:rows, :], power[:rows, :], ALU.pow).then_inc(rstd_a_ready[s], 1)

            def before():
                for s in range(2):
                    norm_a(0, s, P)

            def step(j, slots, rows, next_slots, next_rows):
                def link(instruction, s, step):
                    instruction.then_inc(m_step[s], 1)
                    pool.wait_ge(m_step[s], START + j * 3 + step)

                for s in next_slots:
                    norm_a(j + 1, s, next_rows)
                for s in slots:
                    pool.wait_ge(mean_m_ready[s], START + (j + 1) * 2)
                    link(pool.tensor_tensor(mean_m[s][:rows, 0:1], mean_m[s][:rows, 0:1], mean_m[s][:rows, 1:2], ALU.add), s, 1)
                    apart(pool)
                    link(pool.tensor_scalar(mean_m[s][:rows, 0:1], mean_m[s][:rows, 0:1], NORM_EPS, None, ALU.add), s, 2)
                    pool.wait_ge(h_ready[s], START + j)
                    link(pool.tensor_tensor(rstd_m[s][:rows, :], mean_m[s][:rows, 0:1], power[:rows, 0:1], ALU.pow), s, 3)
                    apart(pool)
                    pool.tensor_scalar(rstd_m[s][:rows, :], rstd_m[s][:rows, :], 1.0 / W_SCALE, None, ALU.mult).then_inc(rstd_m_ready[s], 1)

            iterations(pool, before, step)

        @block.scalar
        def _(act):
            def hi(j, stage, s, n, out, rows):
                c = chunk(j, stage, s, n)
                act.wait_ge(turned, START + c + 1)
                blocks = out.shape[1]
                act.activation(out, T[n % 2][:, :blocks * P].rearrange("p (n t) -> p n t", t=P)[:, :, :rows], ACT.Copy).then_inc(hi_ready, 1)

            def prepare(q, s, rows):
                act.wait_ge(share_asked[s], START + q + 1)
                act.activation(share[s][:rows, :, :], share[s][:rows, :, :], ACT.Exp).then_inc(share_made[s], 1)
                act.wait_ge(early_loaded[s], START + (q + 1) * 5 * 16)
                act.wait_ge(rstd_a_ready[s], START + q)
                for h in range(HEADS):
                    act.activation(junk[:rows, :GLA_DV], oa[s][:rows, h, :], ACT.Square, scale=GLA_DV ** -0.5,
                                   accum_out=mean_a[s][:rows, h:h + 1]).then_inc(mean_a_ready[s], 1)
                    act.wait_ge(mean_a_ready[s], START + q * HEADS + h + 1)
                act.activation(gg[s][:rows, :, :], gg[s][:rows, :, :], ACT.Silu).then_inc(silu_ready[s], 1)
                act.activation(dg[s][:rows, :, :], dg[s][:rows, :, :], ACT.Silu).then_inc(silu_ready[s], 1)

            def keep_z(j, s, rows):
                act.wait_ge(y_made[s], START + j + 1)
                act.wait_ge(proj_made[s], START + j + 1)
                for n in range(3):
                    hi(j, "z", s, n, zT[s][0][:, 4 * n:4 * n + 4, :rows], rows)
                hi(j, "z", s, 3, peT[s][0][:, :, :rows], rows)

            def before():
                for s in range(2):
                    prepare(0, s, P)
                for s in range(2):
                    keep_z(-1, s, P)

            def step(j, slots, rows, next_slots, next_rows):
                for s in slots:
                    act.wait_ge(late_loaded[s], START + (j + 1) * 3 * 16)
                    act.activation(ga[s][:rows, :], ga[s][:rows, :], ACT.Sigmoid).then_inc(gates_ready[s], 1)
                    act.activation(gb[s][:rows, :], gb[s][:rows, :], ACT.Sigmoid).then_inc(gates_ready[s], 1)

                def keep_merged(s):
                    act.wait_ge(gate_made[s], START + j)
                    for n in range(2):
                        hi(j, "m", s, n, mT[s][0][:, 4 * n:4 * n + 4, :rows], rows)

                def square_out(s):
                    act.wait_ge(out_made[s], START + j + 1)
                    for n in range(2):
                        act.activation(junk[:rows, :], OUT[s][n][:rows, :], ACT.Square, scale=D_MODEL ** -0.5 / W_SCALE,
                                       accum_out=mean_m[s][:rows, n:n + 1]).then_inc(mean_m_ready[s], 1)
                        act.wait_ge(mean_m_ready[s], START + j * 2 + n + 1)

                def keep_h(s):
                    for n in range(2):
                        hi(j, "h", s, n, mT[s][0][:, 4 * n:4 * n + 4, :rows], rows)

                def gate(s):
                    act.wait_ge(gate_made[s], START + j + 1)
                    act.wait_ge(h_ready[s], START + j + 1)
                    for n in range(2):
                        act.activation(gb[s][:rows, n * BANK:(n + 1) * BANK], GATE[s][n][:rows, :], ACT.Sigmoid,
                                       scale=1.0 / W_SCALE).then_inc(gate_ready[s], 1)

                keep_merged(0)
                for s in next_slots:
                    prepare(j + 1, s, next_rows)
                if 1 in slots:
                    keep_merged(1)
                square_out(0)
                keep_h(0)
                if 1 in slots:
                    square_out(1)
                if 0 in next_slots:
                    keep_z(j, 0, next_rows)
                gate(0)
                if 1 in slots:
                    keep_h(1)
                if 1 in next_slots:
                    keep_z(j, 1, next_rows)
                if 1 in slots:
                    gate(1)

            iterations(act, before, step)

        @block.vector
        def _(dve):
            dve.wait_ge(g_loaded, START + 16)

            def lo(j, stage, s, n, out, part, rows):
                c = chunk(j, stage, s, n)
                dve.wait_ge(hi_ready, START + c + 1)
                blocks = out.shape[1]
                dve.tensor_tensor(out, T[n % 2][:, :blocks * P].rearrange("p (n t) -> p n t", t=P)[:, :, :rows], part,
                                  ALU.subtract).then_inc(lo_ready, 1)

            PREPARE = 10

            def prepare(q, s, rows):
                done = [0]

                def link(instruction):
                    done[0] += 1
                    instruction.then_inc(prepare_step[s], 1)
                    dve.wait_ge(prepare_step[s], START + q * PREPARE + done[0])

                negmax = og[s][:rows, :, HD].rearrange("p (g h) -> p g h", h=HEADS)
                sums = og[s][:rows, :, HD + 1].rearrange("p (g h) -> p g h", h=HEADS)
                dve.wait_ge(early_loaded[s], START + (q + 1) * 5 * 16)
                link(dve.tensor_tensor(least[s][:rows, :], negmax[:, 0, :], negmax[:, 1, :], ALU.min))
                link(dve.tensor_tensor(least[s][:rows, :], least[s][:rows, :], negmax[:, 2, :], ALU.min))
                for g in range(GROUPS):
                    last = dve.tensor_tensor(share[s][:rows, g, :], least[s][:rows, :], negmax[:, g, :], ALU.subtract)
                last.then_inc(share_asked[s], 1)
                dve.wait_ge(share_made[s], START + q + 1)
                link(dve.tensor_tensor(shareL[s][:rows, :, :], share[s][:rows, :, :], sums, ALU.mult))
                link(dve.tensor_tensor(total[s][:rows, :], shareL[s][:rows, 0, :], shareL[s][:rows, 1, :], ALU.add))
                link(dve.tensor_tensor(total[s][:rows, :], total[s][:rows, :], shareL[s][:rows, 2, :], ALU.add))
                link(dve.reciprocal(total[s][:rows, :], total[s][:rows, :]))
                for g in range(GROUPS):
                    last = dve.tensor_tensor(share[s][:rows, g, :], share[s][:rows, g, :], total[s][:rows, :], ALU.mult)
                link(last)
                flat = share[s][:rows, :, :].rearrange("p g h -> p (g h)")
                link(dve.tensor_tensor(og[s][:rows, :, :HD], og[s][:rows, :, :HD],
                                       flat.unsqueeze(2).to_broadcast([rows, GROUPS * HEADS, HD]), ALU.mult))
                ob = og[s][:rows, 0:HEADS, :HD]
                link(dve.tensor_tensor(ob, ob, og[s][:rows, HEADS:2 * HEADS, :HD], ALU.add))
                link(dve.tensor_tensor(ob, ob, og[s][:rows, 2 * HEADS:3 * HEADS, :HD], ALU.add))
                dve.wait_ge(silu_ready[s], START + (q + 1) * 2)
                dve.tensor_tensor(dg[s][:rows, :, :], ob, dg[s][:rows, :, :], ALU.mult)
                dve.wait_ge(rstd_a_ready[s], START + q + 1)
                for h in range(HEADS):
                    last = dve.scalar_tensor_tensor(out=oa[s][:rows, h, :], in0=oa[s][:rows, h, :], scalar=rstd_a[s][:rows, h:h + 1],
                                                    in1=gg[s][:rows, h, :], op0=ALU.mult, op1=ALU.mult)
                last.then_inc(z_ready[s], 1)
                assert done[0] == PREPARE

            def keep_z(j, s, rows):
                for n in range(3):
                    lo(j, "z", s, n, zT[s][1][:, 4 * n:4 * n + 4, :rows], zT[s][0][:, 4 * n:4 * n + 4, :rows], rows)
                lo(j, "z", s, 3, peT[s][1][:, :, :rows], peT[s][0][:, :, :rows], rows)

            def before():
                for s in range(2):
                    prepare(0, s, P)
                for s in range(2):
                    keep_z(-1, s, P)

            def step(j, slots, rows, next_slots, next_rows):
                def merge(s):
                    dve.wait_ge(y_made[s], START + j + 1)
                    dve.wait_ge(gates_ready[s], START + (j + 1) * 2)
                    for n in range(2):
                        part = slice(n * BANK, (n + 1) * BANK)
                        dve.scalar_tensor_tensor(out=ga[s][:rows, part], in0=YA[s][n][:rows, :], scalar=1.0 / W_SCALE, in1=ga[s][:rows, part],
                                                 op0=ALU.mult, op1=ALU.mult)
                        last = dve.scalar_tensor_tensor(out=gb[s][:rows, part], in0=YB[s][n][:rows, :], scalar=1.0 / W_SCALE,
                                                        in1=gb[s][:rows, part], op0=ALU.mult, op1=ALU.mult)
                    last.then_inc(products_gated[s], 1)
                    dve.wait_ge(products_gated[s], START + j + 1)
                    dve.tensor_tensor(ga[s][:rows, :], ga[s][:rows, :], gb[s][:rows, :], ALU.add).then_inc(merged[s], 1)

                def keep(stage, s):
                    for n in range(2):
                        lo(j, stage, s, n, mT[s][1][:, 4 * n:4 * n + 4, :rows], mT[s][0][:, 4 * n:4 * n + 4, :rows], rows)

                def add_out(s):
                    dve.wait_ge(rstd_m_ready[s], START + j + 1)
                    for n in range(2):
                        part = slice(n * BANK, (n + 1) * BANK)
                        last = dve.scalar_tensor_tensor(out=gb[s][:rows, part], in0=OUT[s][n][:rows, :], scalar=rstd_m[s][:rows, :],
                                                        in1=g_post_sb[:rows, part], op0=ALU.mult, op1=ALU.mult)
                    last.then_inc(out_scaled[s], 1)
                    dve.wait_ge(out_scaled[s], START + j + 1)
                    dve.tensor_tensor(x[s][:rows, :], x[s][:rows, :], gb[s][:rows, :], ALU.add).then_inc(h_ready[s], 1)

                def add_ple(s):
                    dve.wait_ge(proj_made[s], START + j + 1)
                    dve.wait_ge(gate_ready[s], START + (j + 1) * 2)
                    for n in range(2):
                        part = slice(n * BANK, (n + 1) * BANK)
                        last = dve.scalar_tensor_tensor(out=gb[s][:rows, part], in0=PROJ[s][n][:rows, :], scalar=1.0 / W_SCALE,
                                                        in1=gb[s][:rows, part], op0=ALU.mult, op1=ALU.mult)
                    last.then_inc(ple_gated[s], 1)
                    dve.wait_ge(ple_gated[s], START + j + 1)
                    dve.tensor_tensor(x[s][:rows, :], x[s][:rows, :], gb[s][:rows, :], ALU.add).then_inc(y_ready[s], 1)

                merge(0)
                keep("m", 0)
                if 0 in next_slots:
                    prepare(j + 1, 0, next_rows)
                if 1 in slots:
                    merge(1)
                if 1 in next_slots:
                    prepare(j + 1, 1, next_rows)
                if 1 in slots:
                    keep("m", 1)
                add_out(0)
                keep("h", 0)
                if 0 in next_slots:
                    keep_z(j, 0, next_rows)
                if 1 in slots:
                    add_out(1)
                    keep("h", 1)
                add_ple(0)
                if 1 in next_slots:
                    keep_z(j, 1, next_rows)
                if 1 in slots:
                    add_ple(1)

            iterations(dve, before, step)

        @block.tensor
        def _(pe):
            def turn(j, stage, s, n, blocks, rows):
                c = chunk(j, stage, s, n)
                if not isinstance(c, int) or c > 1:
                    pe.wait_ge(lo_ready, START + c - 1)
                for i, src in enumerate(blocks):
                    last = pe.transpose(T[n % 2][:, i * P:i * P + rows], src, identity[:rows, :rows])
                last.then_inc(turned, 1)

            def turn_z(j, s, rows):
                pe.wait_ge(z_ready[s], START + j + 2)
                for n in range(2):
                    turn(j, "z", s, n, [oa[s][:rows, 2 * n + i // 2, i % 2 * P:(i % 2 + 1) * P] for i in range(4)], rows)
                turn(j, "z", s, 2, [dg[s][:rows, i, :] for i in range(4)], rows)
                turn(j, "z", s, 3, [pe_in[s][:rows, i * P:(i + 1) * P] for i in range(2)], rows)

            def turn_wide(j, stage, s, src, rows):
                for n in range(2):
                    turn(j, stage, s, n, [src[s][:rows, (4 * n + i) * P:(4 * n + i + 1) * P] for i in range(4)], rows)

            def product(out, parts, name, slices, rows, signal=None):
                hi, lo = parts
                at = first[name]
                for k in range(slices):
                    for a, b in ((hi, w_hi), (hi, w_lo), (lo, w_hi)):
                        for n in range(2):
                            last = pe.matmul(out[n][:rows, :], a[:, k, :rows], b[:, at + k, n * BANK:(n + 1) * BANK],
                                             start=(k == 0 and a is hi and b is w_hi), stop=(k == slices - 1 and a is lo))
                if signal is not None:
                    last.then_inc(signal, 1)

            def before():
                for s in range(2):
                    turn_z(-1, s, P)

            def step(j, slots, rows, next_slots, next_rows):
                both = 1 in slots

                def gla(s):
                    product(YA[s], zT[s], "gla", GLA_VAL // P, rows)

                def dil(s):
                    product(YB[s], [part[:, GLA_VAL // P:, :] for part in zT[s]], "dil", WIDTH // P, rows, y_made[s])

                def turn_merged(s):
                    pe.wait_ge(merged[s], START + j + 1)
                    turn_wide(j, "m", s, ga, rows)

                def out(s):
                    pe.wait_ge(lo_ready, START + chunk(j, "m", s, 1) + 1)
                    product(OUT[s], mT[s], "out", K_TILES, rows, out_made[s])

                def turn_h(s):
                    pe.wait_ge(h_ready[s], START + j + 1)
                    turn_wide(j, "h", s, x, rows)

                def gate(s):
                    pe.wait_ge(lo_ready, START + chunk(j, "h", s, 1) + 1)
                    product(GATE[s], mT[s], "gate", K_TILES, rows, gate_made[s])

                def proj(s):
                    product(PROJ[s], peT[s], "proj", PLE // P, rows, proj_made[s])

                pe.wait_ge(lo_ready, START + chunk(j, "m", 0, 0))
                gla(0)
                pe.wait_ge(y_ready[1], START + (j if both else PAIRS))
                dil(0)
                if both:
                    gla(1)
                turn_merged(0)
                if both:
                    dil(1)
                    out(0)
                    turn_merged(1)
                    proj(0)
                    out(1)
                else:
                    proj(0)
                    out(0)
                turn_h(0)
                if 0 in next_slots:
                    turn_z(j, 0, next_rows)
                gate(0)
                if both:
                    turn_h(1)
                    proj(1)
                if 1 in next_slots:
                    turn_z(j, 1, next_rows)
                if both:
                    pe.wait_ge(y_ready[0], START + j + 1)
                    gate(1)

            iterations(pe, before, step)


def build(nc, a, outs):
    y_prompt, y_sample, state_prompt, state_sample = outs[:4]
    kv_prompt, kv_sample = outs[4:7], outs[7:10]
    caches = [a["cache_kv_w128"], a["cache_kv_w512"], a["cache_kv_w2048"]]
    U = nc.dram_tensor("U", (TOKENS, U_WIDTH), F32).ap()
    OG = nc.dram_tensor("OG", (TOKENS, GROUPS, HEADS * (HD + 2)), F32).ap()
    OA = nc.dram_tensor("OA", (TOKENS, GLA_VAL), F32).ap()
    L = nc.dram_tensor("L", (LOWRANK + 1, TOKENS), F32).ap()
    weights = [("gla", a["w_gla_branch"]), ("dil", a["w_dil_branch"]), ("out", a["w_out"]),
               ("gate", a["w_ple_gate"]), ("proj", a["w_ple_proj"])]
    core = Core(nc)
    with ExitStack() as whole:
        sb, _, _ = core.bind(whole)
        identity = sb("identity", [P, P])
        with ExitStack() as until_projected:
            sb, sem, _ = core.bind(until_projected)
            xn_hi = sb("xn_hi", [P, K_TILES, TOKENS], F16)
            xn_lo = sb("xn_lo", [P, K_TILES, TOKENS], F16)
            raw = [sb(f"raw{s}", [P, K_TILES, BANK]) for s in range(2)]
            raw_loaded = [sem(f"raw_loaded{s}") for s in range(2)]
            w_view = a["w_in"][0].rearrange("(k p) n -> p k n", p=P)
            normalize_inputs(core, a["x_prompt"], a["x_sample"], a["g_pre"], w_view, raw, raw_loaded, identity, xn_hi, xn_lo)
            project_inputs(core, w_view, raw, raw_loaded, xn_hi, xn_lo, U, L, list(zip(caches, kv_sample)))
        prompt_windows(core, U, a["window_mask"], identity, OG, kv_prompt, kv_sample)
        sample_windows(core, U, caches, a["sample_mask"], identity, OG)
        cutter = Cutter(core, whole, weights, a["g_gla_norm"], shared=("out", "gate"))
        with ExitStack() as while_cutting:
            gla_recurrence(core, U, 0, GLA_CHUNK, 2, SEQ // (2 * GLA_CHUNK), None, state_prompt[0], L, a["w_gla_lr"], a["b_gla_lr"],
                           a["causal_prompt"], a["starts_prompt"], identity, OA, cutter.begin(while_cutting))
        gla_recurrence(core, U, SEQ, DEC_SEQ, 1, DEC_BATCH, a["state_gla"][0], state_sample[0], L, a["w_gla_lr"], a["b_gla_lr"],
                       a["causal_sample"], a["starts_sample"], identity, OA)
        mix_outputs(core, U, OG, OA, a["x_prompt"], a["x_sample"], a["p_prompt"], a["p_sample"], cutter.hi, cutter.lo, cutter.first,
                    a["g_post"], identity, y_prompt, y_sample)


def constants():
    return {"window_mask": window_mask(), "sample_mask": sample_mask(),
            "causal_prompt": causal_mask(2 * GLA_CHUNK), "causal_sample": causal_mask(DEC_SEQ),
            "starts_prompt": scan_starts(GLA_CHUNK, 2), "starts_sample": scan_starts(DEC_SEQ, 1)}


_INS = ["x_prompt", "x_sample", "state_gla", "cache_kv_w128", "cache_kv_w512", "cache_kv_w2048", "p_prompt", "p_sample",
        "g_pre", "g_post", "w_in", "w_gla_lr", "b_gla_lr", "g_gla_norm", "w_gla_branch", "w_dil_branch", "w_out",
        "w_ple_proj", "w_ple_gate"]
_OUTS = [(1, SEQ, D_MODEL), (DEC_BATCH, DEC_SEQ, D_MODEL), (1, 1, HEADS, GLA_DK, GLA_DV),
         (1, DEC_BATCH, HEADS, GLA_DK, GLA_DV)] \
    + [(1, 1, w, 2, HEADS, HD) for w, _ in WINDOWS] + [(1, DEC_BATCH, w, 2, HEADS, HD) for w, _ in WINDOWS]


def kernel(**inputs):
    import concourse.bacc as _bacc
    from concourse.bass_utils import run_bass_kernel_spmd as _run

    nc = _bacc.Bacc("TRN2", target_bir_lowering=False, num_devices=1)
    given = {name: np.ascontiguousarray(inputs[name]) for name in _INS} | constants()
    arrays, a = {}, {}
    for name, value in given.items():
        arrays[f"in_{name}"] = value
        a[name] = nc.dram_tensor(f"in_{name}", value.shape, mybir.dt.from_np(value.dtype), kind="ExternalInput").ap()
    outs = [nc.dram_tensor(f"out_{i}", shape, F32, kind="ExternalOutput").ap() for i, shape in enumerate(_OUTS)]
    build(nc, a, outs)
    r = _run(nc, [arrays], core_ids=[0])
    return tuple(r.results[0][f"out_{i}"] for i in range(len(_OUTS)))
```
